# Optimizing a Trainium2 kernel written in Bass

```python
import jax
import jax.numpy as jnp
from jax import lax
import numpy as np

D_MODEL = 1024
BATCH = 1
SEQ = 512
DEPTH = 1

CHUNK = 64
N_META = 16
PAD_FRONT = (-N_META) % CHUNK
CONV_DIM = D_MODEL
CONV_WIDTH = 31
M_HEADS = 4
M_DV = D_MODEL // M_HEADS
M_DK = M_DV // 2
M_DIM = M_HEADS * M_DV
QK_SCALE = M_DK ** -0.5
N_EXPERTS = 32
TOP_K = 4
D_FF = D_MODEL
SWIGLU_ALPHA = 1.702
SWIGLU_LIMIT = 7.0
MOE_BLOCK = 128
NORM_EPS = 1e-5
NEG_GATE = -1.0e4

GLU_OFF = 0
Q_OFF = GLU_OFF + 2 * CONV_DIM
K_OFF = Q_OFF + M_HEADS * M_DK
V_OFF = K_OFF + M_HEADS * M_DK
I_OFF = V_OFF + M_DIM
F_OFF = I_OFF + M_HEADS
O_OFF = F_OFF + M_HEADS
GC_OFF = O_OFF + M_DIM
GM_OFF = GC_OFF + D_MODEL
N_IN = GM_OFF + D_MODEL

kernel_name = 'hybrid_conformer_mlstm_moe_block'

def rms_norm(x, g):
    xf = x.astype(jnp.float32)
    y = xf * lax.rsqrt(jnp.mean(xf * xf, axis=-1, keepdims=True) + NORM_EPS)
    return (y * g.astype(jnp.float32)).astype(x.dtype)

def layer_norm(x, g, b):
    xf = x.astype(jnp.float32)
    mu = jnp.mean(xf, axis=-1, keepdims=True)
    var = jnp.mean(jnp.square(xf - mu), axis=-1, keepdims=True)
    y = (xf - mu) * lax.rsqrt(var + NORM_EPS)
    return (y * g.astype(jnp.float32) + b.astype(jnp.float32)).astype(x.dtype)

def conformer_conv(zc, dw_w, dw_b, ln_g, ln_b, pw_w, pw_b):
    a, gate = jnp.split(zc, 2, axis=-1)
    y = a * jax.nn.sigmoid(gate)
    y = lax.conv_general_dilated(
        y, dw_w[:, None, :].astype(y.dtype), window_strides=(1,),
        padding=[(CONV_WIDTH - 1, 0)], dimension_numbers=('NWC', 'WIO', 'NWC'),
        feature_group_count=CONV_DIM) + dw_b
    y = jax.nn.silu(layer_norm(y, ln_g, ln_b))
    return y @ pw_w + pw_b

def mlstm_chunkwise(q, k, v, ig, lf):
    bsz, nh, length, dk = q.shape
    dv = v.shape[-1]
    nc = length // CHUNK
    q = q.reshape(bsz, nh, nc, CHUNK, dk)
    k = k.reshape(bsz, nh, nc, CHUNK, dk)
    v = v.reshape(bsz, nh, nc, CHUNK, dv)
    ig = ig.reshape(bsz, nh, nc, CHUNK)
    b = jnp.cumsum(lf.reshape(bsz, nh, nc, CHUNK), axis=-1)
    g = b[..., -1]
    a = g[..., None] - b + ig
    m_loc = jnp.max(a, axis=-1)
    w = jnp.exp(a - m_loc[..., None])
    c_loc = jnp.einsum('bhcs,bhcsv,bhcsk->bhcvk', w, v, k)
    n_loc = jnp.einsum('bhcs,bhcsk->bhck', w, k)

    def step(carry, inp):
        c_st, n_st, m_st = carry
        c_l, n_l, m_l, g_c = inp
        m_new = jnp.maximum(g_c + m_st, m_l)
        s_old = jnp.exp(g_c + m_st - m_new)
        s_loc = jnp.exp(m_l - m_new)
        c_new = s_old[..., None, None] * c_st + s_loc[..., None, None] * c_l
        n_new = s_old[..., None] * n_st + s_loc[..., None] * n_l
        return (c_new, n_new, m_new), (c_st, n_st, m_st)

    init = (jnp.zeros((bsz, nh, dv, dk), jnp.float32),
            jnp.zeros((bsz, nh, dk), jnp.float32),
            jnp.zeros((bsz, nh), jnp.float32))
    xs = (jnp.moveaxis(c_loc, 2, 0), jnp.moveaxis(n_loc, 2, 0),
          jnp.moveaxis(m_loc, 2, 0), jnp.moveaxis(g, 2, 0))
    _, (c_prev, n_prev, m_prev) = lax.scan(step, init, xs)
    c_prev = jnp.moveaxis(c_prev, 0, 2)
    n_prev = jnp.moveaxis(n_prev, 0, 2)
    m_prev = jnp.moveaxis(m_prev, 0, 2)

    causal = jnp.tril(jnp.ones((CHUNK, CHUNK), dtype=bool))
    d_log = jnp.where(causal, b[..., :, None] - b[..., None, :] + ig[..., None, :], -jnp.inf)
    inter_log = b + m_prev[..., None]
    m_t = jnp.maximum(inter_log, jnp.max(d_log, axis=-1))
    s = jnp.einsum('bhctk,bhcsk->bhcts', q, k) * jnp.exp(d_log - m_t[..., None])
    inter_sc = jnp.exp(inter_log - m_t)
    num = (jnp.einsum('bhcts,bhcsv->bhctv', s, v)
           + inter_sc[..., None] * jnp.einsum('bhctk,bhcvk->bhctv', q, c_prev))
    den = jnp.sum(s, axis=-1) + inter_sc * jnp.einsum('bhctk,bhck->bhct', q, n_prev)
    h = num / jnp.maximum(jnp.abs(den), jnp.exp(-m_t))[..., None]
    return h.reshape(bsz, nh, length, dv)

def mlstm_branch(z, norm_g, out_w):
    bsz, length, _ = z.shape

    def to_heads(cols, dh):
        return cols.reshape(bsz, length, M_HEADS, dh).transpose(0, 2, 1, 3).astype(jnp.float32)

    q = to_heads(z[..., Q_OFF:K_OFF], M_DK) * QK_SCALE
    k = to_heads(z[..., K_OFF:V_OFF], M_DK)
    v = to_heads(z[..., V_OFF:I_OFF], M_DV)
    ig = z[..., I_OFF:F_OFF].astype(jnp.float32).transpose(0, 2, 1)
    lf = jax.nn.log_sigmoid(z[..., F_OFF:O_OFF].astype(jnp.float32)).transpose(0, 2, 1)
    pad4 = ((0, 0), (0, 0), (PAD_FRONT, 0), (0, 0))
    pad3 = pad4[:3]
    h = mlstm_chunkwise(jnp.pad(q, pad4), jnp.pad(k, pad4), jnp.pad(v, pad4),
                        jnp.pad(ig, pad3, constant_values=NEG_GATE), jnp.pad(lf, pad3))
    h = h[:, :, PAD_FRONT:].transpose(0, 2, 1, 3)
    h = h * lax.rsqrt(jnp.mean(h * h, axis=-1, keepdims=True) + NORM_EPS)
    h = h.reshape(bsz, length, M_DIM) * norm_g.astype(jnp.float32)
    o = jax.nn.sigmoid(z[..., O_OFF:GC_OFF])
    return (o * h.astype(z.dtype)) @ out_w

def moe_ffn(xt, router_w, router_b, w1, b1, w2, b2):
    n_tok, d = xt.shape
    logits = xt.astype(jnp.float32) @ router_w.astype(jnp.float32) + router_b.astype(jnp.float32)
    top_val, top_idx = lax.top_k(logits, TOP_K)
    gates = jax.nn.softmax(top_val, axis=-1).astype(xt.dtype)
    n_asg = n_tok * TOP_K
    flat_e = top_idx.reshape(-1)
    order = jnp.argsort(flat_e)
    sorted_e = flat_e[order]
    counts = jnp.bincount(flat_e, length=N_EXPERTS)
    padded = (counts + MOE_BLOCK - 1) // MOE_BLOCK * MOE_BLOCK
    grp_start = jnp.cumsum(counts) - counts
    pad_end = jnp.cumsum(padded)
    pad_start = pad_end - padded
    dest_sorted = (pad_start[sorted_e] + jnp.arange(n_asg) - grp_start[sorted_e]).astype(jnp.int32)
    n_blocks = -(-n_asg // MOE_BLOCK) + N_EXPERTS
    slot_tok = jnp.full((n_blocks * MOE_BLOCK,), n_tok, jnp.int32).at[dest_sorted].set(
        (order // TOP_K).astype(jnp.int32))
    blk_e = jnp.minimum(jnp.searchsorted(pad_end, jnp.arange(n_blocks) * MOE_BLOCK, side='right'),
                        N_EXPERTS - 1)
    x_ext = jnp.concatenate([xt, jnp.zeros((1, d), xt.dtype)], axis=0)
    xs = x_ext[slot_tok].reshape(n_blocks, MOE_BLOCK, d)

    def expert_block(args):
        xb, e = args
        hcat = xb @ w1[e] + b1[e]
        h_glu, h_lin = jnp.split(hcat, 2, axis=-1)
        h_glu = jnp.minimum(h_glu, SWIGLU_LIMIT)
        h_lin = jnp.clip(h_lin, -SWIGLU_LIMIT, SWIGLU_LIMIT)
        act = h_glu * jax.nn.sigmoid(SWIGLU_ALPHA * h_glu) * (h_lin + 1.0)
        return act @ w2[e] + b2[e]

    ys = lax.map(expert_block, (xs, blk_e)).reshape(n_blocks * MOE_BLOCK, d)
    dest = jnp.zeros((n_asg,), jnp.int32).at[order].set(dest_sorted).reshape(n_tok, TOP_K)
    return jnp.einsum('nk,nkd->nd', gates, ys[dest])

def setup_inputs(seed: int = 0) -> dict:
    key = jax.random.key(seed)
    ks = jax.random.split(key, 24)
    D = D_MODEL
    nrm = jax.random.normal
    b_in = 0.02 * nrm(ks[4], (DEPTH, N_IN), jnp.float32)
    b_in = b_in.at[:, F_OFF:O_OFF].add(jnp.linspace(3.0, 6.0, M_HEADS))
    return {
        'x': nrm(ks[0], (BATCH, SEQ, D), jnp.float32),
        'meta_tokens': nrm(ks[1], (N_META, D), jnp.float32),
        'norm_mix_g': 1.0 + 0.02 * nrm(ks[2], (DEPTH, D), jnp.float32),
        'w_in': nrm(ks[3], (DEPTH, D, N_IN), jnp.float32) * D ** -0.5,
        'b_in': b_in,
        'conv_dw_w': nrm(ks[5], (DEPTH, CONV_WIDTH, CONV_DIM), jnp.float32) * CONV_WIDTH ** -0.5,
        'conv_dw_b': 0.02 * nrm(ks[6], (DEPTH, CONV_DIM), jnp.float32),
        'conv_ln_g': 1.0 + 0.02 * nrm(ks[7], (DEPTH, CONV_DIM), jnp.float32),
        'conv_ln_b': 0.02 * nrm(ks[8], (DEPTH, CONV_DIM), jnp.float32),
        'conv_pw_w': nrm(ks[9], (DEPTH, CONV_DIM, D), jnp.float32) * CONV_DIM ** -0.5,
        'conv_pw_b': 0.02 * nrm(ks[10], (DEPTH, D), jnp.float32),
        'mlstm_norm_g': 1.0 + 0.02 * nrm(ks[11], (DEPTH, M_DIM), jnp.float32),
        'mlstm_out_w': nrm(ks[12], (DEPTH, M_DIM, D), jnp.float32) * M_DIM ** -0.5,
        'w_out': nrm(ks[13], (DEPTH, D, D), jnp.float32) * D ** -0.5,
        'norm_ffn_g': 1.0 + 0.02 * nrm(ks[14], (DEPTH, D), jnp.float32),
        'router_w': nrm(ks[15], (DEPTH, D, N_EXPERTS), jnp.float32) * D ** -0.5,
        'router_b': 0.01 * nrm(ks[16], (DEPTH, N_EXPERTS), jnp.float32),
        'expert_w1': nrm(ks[17], (DEPTH, N_EXPERTS, D, 2 * D_FF), jnp.float32) * D ** -0.5,
        'expert_b1': 0.02 * nrm(ks[18], (DEPTH, N_EXPERTS, 2 * D_FF), jnp.float32),
        'expert_w2': nrm(ks[19], (DEPTH, N_EXPERTS, D_FF, D), jnp.float32) * D_FF ** -0.5,
        'expert_b2': 0.02 * nrm(ks[20], (DEPTH, N_EXPERTS, D), jnp.float32),
        'final_norm_g': 1.0 + 0.02 * nrm(ks[21], (D,), jnp.float32),
    }

def reference(x, meta_tokens, norm_mix_g, w_in, b_in, conv_dw_w, conv_dw_b, conv_ln_g, conv_ln_b,
              conv_pw_w, conv_pw_b, mlstm_norm_g, mlstm_out_w, w_out, norm_ffn_g, router_w, router_b,
              expert_w1, expert_b1, expert_w2, expert_b2, final_norm_g):
    bsz, seq, d = x.shape
    meta = jnp.broadcast_to(meta_tokens.astype(x.dtype)[None], (bsz, N_META, d))
    h = jnp.concatenate([meta, x], axis=1)
    for l in range(DEPTH):
        u = rms_norm(h, norm_mix_g[l])
        z = u @ w_in[l] + b_in[l]
        conv_out = conformer_conv(z[..., GLU_OFF:Q_OFF], conv_dw_w[l], conv_dw_b[l], conv_ln_g[l],
                                  conv_ln_b[l], conv_pw_w[l], conv_pw_b[l])
        mlstm_out = mlstm_branch(z, mlstm_norm_g[l], mlstm_out_w[l])
        g_conv = jax.nn.sigmoid(z[..., GC_OFF:GM_OFF])
        g_mlstm = jax.nn.sigmoid(z[..., GM_OFF:N_IN])
        h = h + (g_conv * conv_out + g_mlstm * mlstm_out) @ w_out[l]
        u2 = rms_norm(h, norm_ffn_g[l])
        h = h + moe_ffn(u2.reshape(-1, d), router_w[l], router_b[l], expert_w1[l], expert_b1[l],
                        expert_w2[l], expert_b2[l]).reshape(h.shape)
    return rms_norm(h, final_norm_g)[:, N_META:]


_drawn_inputs = setup_inputs


def setup_inputs(seed=0):
    import zlib

    import numpy as np

    out = dict(_drawn_inputs(seed))
    spreads = {}
    factors = {'expert_b1': 5.495, 'expert_b2': 6.268, 'final_norm_g': 2.746}
    for name, (base, spread) in spreads.items():
        noise = np.random.default_rng([zlib.crc32(name.encode()), seed]).standard_normal(out[name].shape)
        drawn = base * np.exp(spread * noise) if base else spread * noise
        out[name] = jnp.asarray(drawn.astype(out[name].dtype))
    for name, factor in factors.items():
        out[name] = (out[name] * factor).astype(out[name].dtype)
    return out
```

```python
import concourse.bass as bass
from concourse import mybir
from contextlib import ExitStack
import numpy as np

F32 = mybir.dt.float32
F32R = mybir.dt.float32r
BF16 = mybir.dt.bfloat16
I32 = mybir.dt.int32
U32 = mybir.dt.uint32
ACT = mybir.ActivationFunctionType
ALU = mybir.AluOpType
AX = mybir.AxisListType

P = 128
D = 1024
SEQ = 512
META = 16
NT = META + SEQ
HALF = NT // 2
KT = D // P
TT = SEQ // P
HEADS = 4
DV = D // HEADS
DK = DV // 2
VW = DV + 1
CHUNKS = TT + 1
CONV_W = 31
PADL = CONV_W - 1 - META
CIN = PADL + NT
QK_SCALE = DK ** -0.5
EPS = 1e-5
NE = 32
TOPK = 4
DFF = D
ALPHA = 1.702
LIMIT = 7.0
GRP = 256
GT = GRP // P
MASKED = 1.0e30

GATE_OFF = D
Q_OFF = 2 * D
K_OFF = Q_OFF + HEADS * DK
V_OFF = K_OFF + HEADS * DK
I_OFF = V_OFF + D
F_OFF = I_OFF + HEADS
O_OFF = F_OFF + HEADS
GC_OFF = O_OFF + D
GM_OFF = GC_OFF + D
F_ROW = 32
W_ROW, FLOOR_ROW = 32, 64
ROWS = 96

GLU_PAIR, QK_PAIR, V_PAIR, SIG_PAIR, PW_PAIR, OW_PAIR, WO_PAIR = 0, 4, 6, 8, 14, 16, 18

B_A, B_Q, B_SIG, LN_G, LN_B, PW_B, MN_G, DW_B = 0, 16, 24, 48, 56, 64, 72, 80
VEC_ROWS = 88

SLOTS = 96
TG = SLOTS // 32
CG = 4
PASSES = -(-SEQ // SLOTS)
NONE = 1 << 14
RING = 12
W1C = KT
RC = DFF * 2


def chunk_span(c):
    return (0, META) if c == 0 else (META + P * (c - 1), META + P * c)


def hybrid_block(nc, x, meta_tokens, norm_mix_g, w_in, b_in, conv_dw_w, conv_dw_b, conv_ln_g, conv_ln_b,
                 conv_pw_w, conv_pw_b, mlstm_norm_g, mlstm_out_w, w_out, norm_ffn_g, router_w, router_b,
                 expert_w1, expert_b1, expert_w2, expert_b2, final_norm_g, out):
    ctx = ExitStack()
    with ctx:
        def sem(name):
            return ctx.enter_context(nc.semaphore(name))

        base = -(-nc.sbuf_base // 32) * 32
        limit = nc.sbuf_usable_end
        top = [base]

        def at(name, shape, dt, offset):
            return nc.alloc_sbuf_tensor_at(name, shape, dt, offset=offset).ap()

        def size(shape, dt=F32):
            return -(-int(np.prod(shape[1:])) * mybir.dt.size(dt) // 32) * 32

        def take(name, shape, dt=F32):
            off = top[0]
            top[0] += size(shape, dt)
            return at(name, shape, dt, off), off

        chan = size([P, KT, SEQ])
        stage, stage_at = take("stage", [P, 2, KT, GRP])
        w_hi, _ = take("w_hi", [P, 2, KT, GRP], F32R)
        w_lo, _ = take("w_lo", [P, 2, KT, GRP], F32R)
        u_hi, u_hi_at = take("u_hi", [P, KT, NT], F32R)
        gates_at = top[0]
        gates = at("gates", [P, 3 * KT, SEQ], F32, gates_at)
        top[0] += 2 * chan
        conv_in, _ = take("conv_in", [P, KT, CIN])
        u_lo, u_lo_at = take("u_lo", [P, KT, NT], F32R)
        conv, conv_at = take("conv", [P, KT, SEQ])
        q_sb, q_at = take("q_sb", [P, HEADS, SEQ])
        k_sb, _ = take("k_sb", [P, HEADS, NT])
        v_sb, v_at = take("v_sb", [P, TT, HEADS, VW])
        v_meta, _ = take("v_meta", [META, HEADS, VW])
        ring_end = top[0]
        probs, probs_at = take("probs", [P, HEADS, SEQ])
        state, state_at = take("state", [P, HEADS, VW])
        kw_sb, kw_at = take("kw_sb", [P, HEADS, DK])
        h_tok, h_tok_at = take("h_tok", [P, HEADS, DV])
        cols, _ = take("cols", [P, CHUNKS, ROWS])
        decay, _ = take("decay", [P, HEADS, TT])
        ident, _ = take("ident", [P, P])
        mean_w, _ = take("mean_w", [P, P])
        maskpos, _ = take("maskpos", [P, P])
        taps, _ = take("taps", [P, KT, CONV_W])
        vec, _ = take("vec", [P, VEC_ROWS])
        small, _ = take("small", [P, 64])
        assert top[0] <= limit, (top[0], limit)

        x_sb = at("x_sb", [P, TT, D], F32, gates_at)
        g_bc = at("g_bc", [P, D], F32, gates_at + chan)
        meta_sb = at("meta_sb", [META, D], F32, gates_at + chan + size([P, D]))
        square_out = at("square_out", [P, D], F32, gates_at + chan + 2 * size([P, D]))
        vec_rows = at("vec_rows", [VEC_ROWS, P], F32, conv_at)
        tap_rows = at("tap_rows", [CONV_W, D], F32, conv_at + size([P, P]))
        wif = at("wif", [P, KT, P], F32, v_at)
        wif_hi = at("wif_hi", [P, KT, P], F32R, v_at + size([P, KT, P]))
        wif_lo = at("wif_lo", [P, KT, P], F32R, v_at + 2 * size([P, KT, P]))
        rows_at, row = v_at + 3 * size([P, KT, P]), size([HEADS, NT])
        i_row = at("i_row", [HEADS, NT], F32, rows_at)
        f_row = at("f_row", [HEADS, NT], F32, rows_at + row)
        t_row = at("t_row", [HEADS, NT], F32, rows_at + 2 * row)
        keep_row = at("keep_row", [HEADS, NT], F32, q_at)
        b_row = at("b_row", [HEADS, NT], F32, q_at + row)
        e_row = at("e_row", [HEADS, NT], F32, q_at + 2 * row)
        sg = at("sg", [P, 2, HALF], F32, probs_at)
        vb_bc = at("vb_bc", [P, D], F32, probs_at + size([P, D]))
        gate_rows = at("gate_rows", [P, NT], F32, state_at)
        m_row = at("m_row", [HEADS, NT], F32, kw_at)
        inter_row = at("inter_row", [HEADS, NT], F32, kw_at + row)
        squares = at("squares", [P, KT, SEQ], F32, u_hi_at)
        rstd_bc = at("rstd_bc", [P, SEQ], F32, stage_at)
        silu_hi = at("silu_hi", [P, KT, SEQ], F32R, u_hi_at)
        silu_lo = at("silu_lo", [P, KT, SEQ], F32R, conv_at)
        h_hi = at("h_hi", [P, KT, SEQ], F32R, u_lo_at)
        h_lo = at("h_lo", [P, KT, SEQ], F32R, gates_at + chan)
        mix_hi = at("mix_hi", [P, KT, SEQ], F32R, u_hi_at)
        mix_lo = at("mix_lo", [P, KT, SEQ], F32R, gates_at)
        h_res = at("h_res", [P, TT, D], F32, probs_at)
        GC, OG, GM = 0, KT, 2 * KT

        chunk = size([P, RC])
        w1_ring = [at(f"w1_ring{c}", [P, 2, DFF], F32, ring_end - chunk * (c + 1)) for c in range(W1C)]
        w2_ring = [at(f"w2_ring{c}", [P, 2, D], F32, ring_end - chunk * (W1C + c + 1)) for c in range(RING - W1C)]
        assert ring_end - chunk * RING >= gates_at + chan
        low = [gates_at + chan]

        def under_ring(name, shape, dt=F32):
            off = low[0]
            low[0] += size(shape, dt)
            assert low[0] <= ring_end - chunk * RING
            return at(name, shape, dt, off)

        w_router = under_ring("w_router", [P, KT, NE])
        logits = under_ring("logits", [P, TT, NE])
        rb_bc = under_ring("rb_bc", [P, NE])
        top = under_ring("top", [P, TT, 8])
        top_idx = under_ring("top_idx", [P, TT, 8], U32)
        gate_w = under_ring("gate_w", [P, TT, TOPK])
        expert_f = under_ring("expert_f", [P, TT, TOPK])
        gate_sum = under_ring("gate_sum", [P, TT])
        n_passes = under_ring("n_passes", [P, 1], I32)
        count_max = under_ring("count_max", [P, 1])
        over = under_ring("over", [P, 8])
        carrier = under_ring("carrier", [1, 2 + TG])

        ffn_at = [stage_at]

        def in_stage(name, shape, dt=F32):
            off = ffn_at[0]
            ffn_at[0] += size(shape, dt)
            return at(name, shape, dt, off)

        u2 = in_stage("u2", [P, 2, D])
        u2T = in_stage("u2T", [P, KT, P])
        gf_bc = in_stage("gf_bc", [P, D])
        assert ffn_at[0] <= stage_at + 2 * size([P, KT, GRP])
        one_hot = in_stage("one_hot", [P, TT * TOPK, NE])
        picked = in_stage("picked", [P, TT * TOPK, NE])
        mask = in_stage("mask", [P, TT, NE], BF16)
        place = in_stage("place", [P, TT * TOPK])
        dest = in_stage("dest", [P, TT * TOPK], I32)
        code = in_stage("code", [P, TT * TOPK], I32)
        expert_id = in_stage("expert_id", [P, NE])
        earlier = in_stage("earlier", [P, P], BF16)
        all_ones = in_stage("all_ones", [P, P], BF16)
        steps96 = in_stage("steps96", [P, PASSES - 1])
        no_code = in_stage("no_code", [SLOTS, PASSES * NE], I32)
        group_of = in_stage("group_of", [P, 1])
        token_of = in_stage("token_of", [SLOTS, PASSES * NE + 1], I32)
        row_of = in_stage("row_of", [P, TG, PASSES * NE + 1], I32)
        token_now = in_stage("token_now", [SLOTS, 1], I32)
        row_now = in_stage("row_now", [P, TG], I32)
        xs = in_stage("xs", [SLOTS, D])
        xT = in_stage("xT", [P, KT, SLOTS])
        hid = in_stage("hid", [P, TG, 2 * GRP])
        sig = in_stage("sig", [P, TG, GRP])
        act_v = in_stage("act_v", [P, TG, GRP])
        actT = in_stage("actT", [P, KT, SLOTS])
        y_out = in_stage("y_out", [P, TG, GRP])
        bias1 = in_stage("bias1", [P, 2, GRP])
        bias2 = in_stage("bias2", [P, GRP])
        last_g = in_stage("last_g", [P, D])
        assert ffn_at[0] <= gates_at + chan
        y_in = at("y_in", [P, TT, TOPK, D], F32, ring_end - TT * TOPK * size([P, D]))

        u2_dram = nc.dram_tensor("u2_rows", [SEQ, D], F32).ap()
        y_dram = nc.dram_tensor("y_rows", [SEQ * TOPK * CG, GRP], F32).ap()
        table = nc.dram_tensor("slot_table", [PASSES * SLOTS * NE, 1], I32).ap()

        square_sum = small[:, 0:5]
        row_rstd = small[:, 5:10]
        minus_half = small[:, 10:11]
        if_bias = small[:, 11:12]
        m_prev = small[0:HEADS, 12:17]
        minus_m_end = small[0:HEADS, 17:22]
        den_inv = small[:, 22:26]
        head_square = small[:, 26:30]
        head_rstd = small[:, 30:34]
        head_scale = small[:, 34:38]
        q_bias = small[:, 38:42]
        h_square = small[:, 42:46]
        h_rstd = small[:, 46:50]
        f_square = small[:, 50:54]
        f_rstd = small[:, 54:58]

        banks = ctx.enter_context(nc.psum_tensor("banks", [P, 8, 512], F32)).ap()

        x_in = [sem(f"x_in{i}") for i in range(TT)]
        meta_in, g_in, vecs_in, ifw_in, vb_in = sem("meta_in"), sem("g_in"), sem("vecs_in"), sem("ifw_in"), sem("vb_in")
        consts_made, ifw_zeroed = sem("consts_made"), sem("ifw_zeroed")
        squared, rstd_made, scaled = sem("squared"), sem("rstd_made"), sem("scaled")
        u_transposed, u_hi_made, u_lo_made = sem("u_transposed"), sem("u_hi_made"), sem("u_lo_made")
        vecs_transposed, vecs_made = sem("vecs_transposed"), sem("vecs_made")
        ifw_hi_made, ifw_lo_made, if_mm, if_rows = sem("ifw_hi_made"), sem("ifw_lo_made"), sem("if_mm"), sem("if_rows")
        w_in_sem = [sem("w_loaded0"), sem("w_loaded1")]
        w_hi_made = [sem("w_hi_made0"), sem("w_hi_made1")]
        w_lo_made = [sem("w_lo_made0"), sem("w_lo_made1")]
        mm_done = sem("mm_done")
        glu_sig = sem("glu_sig")
        glu_out = [sem("glu_out0"), sem("glu_out1")]
        qk_out, v_out = sem("qk_out"), sem("v_out")
        sig_out = [sem(f"sig_out{t}") for t in range(4)]
        conv_step, dve_step, act_step, pool_step = sem("conv_step"), sem("dve_step"), sem("act_step"), sem("pool_step")
        abs_f, softplus, a_rows, m_rows, gate_rows_made = sem("abs_f"), sem("softplus"), sem("a_rows"), sem("m_rows"), sem("gate_rows_made")
        ln_mm, centered, squares_made, var_made, rstd_bc_made = sem("ln_mm"), sem("centered"), sem("squares_made"), sem("var_made"), sem("rstd_bc_made")
        normed, silu_made, silu_hi_made, silu_lo_made = sem("normed"), sem("silu_made"), sem("silu_hi_made"), sem("silu_lo_made")
        cols_mm, cols_made = sem("cols_mm"), sem("cols_made")
        head_mm, e_made, d_made, head_out = sem("head_mm"), sem("e_made"), sem("d_made"), sem("head_out")
        kt_mm, kw_made, outer_mm, state_out = sem("kt_mm"), sem("kw_made"), sem("outer_mm"), sem("state_out")
        h_mm, den_made, h_squared, h_scaled, tok_made = sem("h_mm"), sem("den_made"), sem("h_squared"), sem("h_scaled"), sem("tok_made")
        ht_mm, ht_gated, h_hi_made, h_lo_made, og_made = sem("ht_mm"), sem("ht_gated"), sem("h_hi_made"), sem("h_lo_made"), sem("og_made")
        pw_out, ow_out, mixed, mix_hi_made, mix_lo_made = sem("pw_out"), sem("ow_out"), sem("mixed"), sem("mix_hi_made"), sem("mix_lo_made")
        res_in, wo_out = sem("res_in"), sem("wo_out")
        stored = sem("stored")
        gf_in, router_in, u2_made, u2_stored = sem("gf_in"), sem("router_in"), sem("u2_made"), [sem(f"u2_stored{i}") for i in range(TT)]
        u2_mm, u2T_made, logits_mm, routed, place_mm = sem("u2_mm"), sem("u2T_made"), sem("logits_mm"), sem("routed"), sem("place_mm")
        moe_consts, mask_made, dest_made, table_set, table_written = sem("moe_consts"), sem("mask_made"), sem("dest_made"), sem("table_set"), sem("table_written")
        table_in, tables_made, passes_made, shifted, gate_exp = sem("table_in"), sem("tables_made"), sem("passes_made"), sem("shifted"), sem("gate_exp")
        ring_in = [sem(f"ring_in{c}") for c in range(RING)]
        ring_used = [sem(f"ring_used{c}") for c in range(RING)]
        xs_in, xs_used, xT_made, idx_step = sem("xs_in"), sem("xs_used"), sem("xT_made"), sem("idx_step")
        hid_mm, glu_made, sig_made, act_made, act_mm, actT_made = sem("hid_mm"), sem("glu_made"), sem("sig_made"), sem("act_made"), sem("act_mm"), sem("actT_made")
        y_mm, y_made, y_stored, b1_in, b2_in, ffn_step = sem("y_mm"), sem("y_made"), sem("y_stored"), sem("b1_in"), sem("b2_in"), sem("ffn_step")
        y_loaded = [sem(f"y_loaded{i}") for i in range(TT)]
        last_g_in, summed, out_made = sem("last_g_in"), sem("summed"), sem("out_made")

        PAIR_TICKS = 8

        def pair_tick(n, k):
            return n * PAIR_TICKS + (PAIR_TICKS + k)

        def w_source(stage_pair, s, j):
            m, a0, b0, step = {
                GLU_PAIR: (w_in[0], 0, GATE_OFF, GRP),
                QK_PAIR: (w_in[0], Q_OFF, K_OFF, GRP),
                V_PAIR: (w_in[0], V_OFF, V_OFF + GRP, 2 * GRP),
                SIG_PAIR: (w_in[0], GC_OFF, GC_OFF + GRP, 2 * GRP),
                PW_PAIR: (conv_pw_w[0], 0, GRP, 2 * GRP),
                OW_PAIR: (mlstm_out_w[0], 0, GRP, 2 * GRP),
                WO_PAIR: (w_out[0], 0, GRP, 2 * GRP),
            }[stage_pair]
            return m.rearrange("(k p) n -> p k n", p=P)[:, :, bass.ds(j * step + (b0 if s else a0), GRP)]

        SIG_OFFS = (GC_OFF, O_OFF, GM_OFF)

        block = ctx.enter_context(nc.Block())

        @block.sync
        def _(sp):
            def load_pair(n, source):
                for s in range(2):
                    sp.wait_ge(w_lo_made[s], n)
                    sp.dma_start(stage[:, s], source(s)).then_inc(w_in_sem[s], 16)

            xt = x[0].rearrange("(i p) d -> i p d", p=P)
            for i in range(TT):
                sp.dma_start(x_sb[:, i], xt[i]).then_inc(x_in[i], 16)
            sp.dma_start(meta_sb, meta_tokens).then_inc(meta_in, 16)
            with sp.Fori(0, 4) as j:
                load_pair(j, lambda s: w_source(GLU_PAIR, s, j))
            for stage_pair in (QK_PAIR, V_PAIR):
                for j in range(2):
                    load_pair(stage_pair + j, lambda s: w_source(stage_pair, s, j))
            win = w_in[0].rearrange("(k p) n -> p k n", p=P)
            for g, off in enumerate(SIG_OFFS):
                for j in range(2):
                    load_pair(SIG_PAIR + 2 * g + j, lambda s: win[:, :, off + (2 * j + s) * GRP:off + (2 * j + s + 1) * GRP])
            for stage_pair in (PW_PAIR, OW_PAIR):
                for j in range(2):
                    load_pair(stage_pair + j, lambda s: w_source(stage_pair, s, j))

            def load_chunk(e, c):
                if c < W1C:
                    src = expert_w1[0, bass.ds(e, 1), P * c:P * (c + 1), :].rearrange("e p (g n) -> p (e g) n", g=2)
                    sp.dma_start(w1_ring[c], src).then_inc(ring_in[c], 16)
                else:
                    m = c - W1C
                    src = expert_w2[0, bass.ds(e, 1), 2 * P * m:2 * P * (m + 1), :].rearrange("e (k p) n -> p (e k) n", p=P)
                    sp.dma_start(w2_ring[m], src).then_inc(ring_in[c], 16)

            sp.wait_ge(h_lo_made, 2 * TT)
            sp.dma_start(h_res, x[0].rearrange("(i p) d -> p i d", p=P)).then_inc(res_in, 16)
            for c in range(4):
                load_chunk(0, c)
            sp.wait_ge(mm_done, pair_tick(PW_PAIR + 1, 8))
            for c in range(4, 6):
                load_chunk(0, c)
            for j in range(2):
                load_pair(WO_PAIR + j, lambda s: w_source(WO_PAIR, s, j))
            sp.wait_ge(mm_done, pair_tick(OW_PAIR + 1, 8))
            sp.wait_ge(mixed, KT)
            for c in range(6, RING):
                load_chunk(0, c)
            sp.dma_start(w_router, router_w[0].rearrange("(k p) e -> p k e", p=P)).then_inc(router_in, 16)
            sp.dma_start(rb_bc, router_b.to_broadcast([P, NE])).then_inc(router_in, 16)
            for s in range(2):
                sp.wait_ge(w_lo_made[s], WO_PAIR + 2)
            sp.dma_start(gf_bc, norm_ffn_g.to_broadcast([P, D])).then_inc(gf_in, 16)
            sp.wait_ge(moe_consts, 1)
            sp.dma_start(table.rearrange("(q i e) o -> i q (e o)", i=SLOTS, e=NE),
                         no_code.rearrange("i (q e) -> i q e", e=NE)).then_inc(table_set, 16)
            for i in range(TT):
                sp.wait_ge(u2_made, i + 1)
                sp.dma_start(u2_dram[P * i:P * (i + 1)], u2[:, i % 2]).then_inc(u2_stored[i], 16)
            sp.wait_ge(table_written, 16 * TT * TOPK)
            by_slot = table.rearrange("(q i e) o -> i q (e o)", i=SLOTS, e=NE)
            sp.dma_start(token_of[:, 0:PASSES * NE].rearrange("i (q e) -> i q e", e=NE), by_slot).then_inc(table_in, 16)
            for g in range(CG):
                for t in range(TG):
                    sp.dma_start(row_of[32 * g:32 * (g + 1), t, 0:PASSES * NE].rearrange("i (q e) -> i q e", e=NE),
                                 by_slot[32 * t:32 * (t + 1)]).then_inc(table_in, 16)
            sp.dma_start(last_g, final_norm_g.rearrange("(a d) -> a d", a=1).to_broadcast([P, D])).then_inc(last_g_in, 16)

            def load_block(n, e):
                for c in range(RING):
                    if c in (W1C - 1, RING - 1):
                        sp.wait_ge(hid_mm if c < W1C else y_mm, n * TG)
                    else:
                        sp.wait_ge(ring_used[c], n)
                    load_chunk(e, c)

            with sp.Fori(1, NE) as e:
                load_block(e, e)
            sp.wait_ge(passes_made, 1)
            passes = sp.value_load(n_passes[0:1, 0:1], min_val=1, max_val=PASSES)
            with sp.If(passes > 1):
                with sp.Fori(1, passes) as q:
                    with sp.Fori(0, NE) as e:
                        load_block(q * NE + e, e)
            sp.wait_ge(y_stored, passes * (16 * TG * NE))
            for i in range(TT):
                sp.dma_start(y_in[:, i], y_dram.rearrange("(i p r) n -> i p (r n)", i=TT, p=P)[i].rearrange(
                    "p (k d) -> p k d", k=TOPK)).then_inc(y_loaded[i], 16)
            for i in range(TT):
                sp.wait_ge(out_made, i + 1)
                sp.dma_start(out[0, P * i:P * (i + 1), :], h_res[:, i]).then_inc(stored, 16)
            sp.wait_ge(stored, 16 * TT)

        @block.gpsimd
        def _(pool):
            steps = [0]

            def chain(ins):
                steps[0] += 1
                ins.then_inc(pool_step, 1)
                pool.wait_ge(pool_step, steps[0])

            nc.gpsimd.memset(minus_half, -0.5).then_inc(mm_done, PAIR_TICKS)
            nc.gpsimd.memset(wif, 0.0).then_inc(ifw_zeroed, 1)
            nc.gpsimd.memset(ident, 0.0)
            chain(nc.gpsimd.memset(maskpos, 0.0))
            nc.gpsimd.affine_select(out=ident, in_=ident, compare_op=ALU.not_equal, fill=1.0, base=0,
                                    pattern=[[-1, P]], channel_multiplier=1).then_inc(consts_made, 1)
            nc.gpsimd.affine_select(out=maskpos, in_=maskpos, compare_op=ALU.is_ge, fill=MASKED, base=0,
                                    pattern=[[1, P]], channel_multiplier=-1).then_inc(consts_made, 1)
            nc.gpsimd.memset(mean_w, 1.0 / D).then_inc(consts_made, 1)
            nc.gpsimd.memset(conv_in[:, :, 0:PADL], 0.0).then_inc(consts_made, 1)
            nc.gpsimd.memset(gate_rows, 0.0).then_inc(consts_made, 1)
            nc.gpsimd.memset(keep_row, 1.0).then_inc(consts_made, 1)
            pool.wait_ge(ifw_zeroed, 1)
            with nc.allow_non_contiguous_dma(reason="4 columns of each row"):
                for off, col in ((I_OFF, 0), (F_OFF, F_ROW)):
                    pool.dma_start(wif[:, :, col:col + HEADS],
                                   w_in[0].rearrange("(k p) n -> p k n", p=P)[:, :, off:off + HEADS]).then_inc(ifw_in, 16)

            def rstd(rows, sums, to, n, done=None):
                chain(nc.gpsimd.tensor_scalar(to, sums, 1.0 / n, EPS, ALU.mult, ALU.add))
                ins = nc.gpsimd.tensor_tensor(to, to, minus_half[0:rows].to_broadcast([rows, to.shape[1]]), ALU.pow)
                if done is None:
                    chain(ins)
                else:
                    ins.then_inc(done, 1)

            for i in range(CHUNKS):
                rows = P if i < TT else META
                pool.wait_ge(squared, i + 1)
                rstd(rows, square_sum[0:rows, i:i + 1], row_rstd[0:rows, i:i + 1], D, rstd_made)
            pool.wait_ge(ifw_hi_made, 1)
            nc.gpsimd.tensor_tensor(wif_lo, wif, wif_hi.bitcast(F32), ALU.subtract).then_inc(ifw_lo_made, 1)

            def split_pair(n):
                for s in range(2):
                    pool.wait_ge(w_hi_made[s], n + 1)
                    pool.wait_ge(mm_done, pair_tick(n, 8 if s else 2) - PAIR_TICKS)
                    nc.gpsimd.tensor_tensor(w_lo[:, s], stage[:, s], w_hi[:, s].bitcast(F32),
                                            ALU.subtract).then_inc(w_lo_made[s], 1)

            with pool.Fori(0, PW_PAIR) as n:
                split_pair(n)
            for t in range(KT):
                pool.wait_ge(sig_out[t % 4], OG // 4 + t // 4 + 1)
                og = gates[:, OG + t]
                nc.gpsimd.tensor_scalar(og, og, vec[:, MN_G + t:MN_G + t + 1], None, ALU.mult).then_inc(og_made, 1)
            split_pair(PW_PAIR)
            pool.wait_ge(var_made, 1)
            chain(nc.gpsimd.tensor_scalar(squares[:, KT - 1], squares[:, KT - 1], EPS, None, ALU.add))
            nc.gpsimd.tensor_tensor(squares[:, KT - 1], squares[:, KT - 1], minus_half.to_broadcast([P, SEQ]),
                                    ALU.pow).then_inc(rstd_bc_made, 1)
            for i in range(TT):
                pool.wait_ge(h_squared, HEADS * (i + 1))
                rstd(P, head_square, head_rstd, DV)
                nc.gpsimd.tensor_tensor(head_scale, head_rstd, den_inv, ALU.mult).then_inc(h_scaled, 1)
            with pool.Fori(PW_PAIR + 1, WO_PAIR + 2) as n:
                split_pair(n)

            pool.wait_ge(mm_done, pair_tick(WO_PAIR + 1, 8))
            nc.gpsimd.memset(no_code, NONE).then_inc(moe_consts, 1)
            nc.gpsimd.iota(code, [[TOPK * P, TT], [1, TOPK]], base=0, channel_multiplier=TOPK)
            nc.gpsimd.iota(expert_id, [[1, NE]], base=0, channel_multiplier=0, allow_small_or_imprecise_dtypes=True)
            chain(nc.gpsimd.iota(steps96, [[SLOTS, PASSES - 1]], base=SLOTS, channel_multiplier=0, allow_small_or_imprecise_dtypes=True))
            for g in range(CG):
                chain(nc.gpsimd.memset(group_of[32 * g:32 * (g + 1)], float(g)))
            nc.gpsimd.memset(all_ones, 1.0)
            nc.gpsimd.memset(carrier, 0.0)
            nc.gpsimd.memset(token_of, NONE)
            nc.gpsimd.memset(row_of, NONE)
            nc.gpsimd.memset(xs, 0.0)
            chain(nc.gpsimd.memset(earlier, 1.0))
            nc.gpsimd.affine_select(out=earlier, in_=earlier, compare_op=ALU.is_gt, fill=0.0, base=0,
                                    pattern=[[1, P]], channel_multiplier=-1).then_inc(moe_consts, 1)
            for i in range(TT):
                pool.wait_ge(squared, CHUNKS + i + 1)
                rstd(P, h_square[:, i:i + 1], h_rstd[:, i:i + 1], D, rstd_made)
            pool.wait_ge(table_set, 16)
            pool.wait_ge(dest_made, 1)
            for m in range(TT * TOPK):
                pool.indirect_dma_start(out=table, out_offset=bass.IndirectOffsetOnAxis(ap=dest[:, m:m + 1], axis=0),
                                        in_=code[:, m:m + 1], in_offset=None).then_inc(table_written, 16)

            pool.wait_ge(tables_made, 2)
            for i in range(TT):
                pool.wait_ge(u2_stored[i], 16)
            IDX = 3 + TG

            def gather(n, copied):
                nc.gpsimd.tensor_copy(token_now, token_of[:, bass.ds(n, 1)]).then_inc(idx_step, 1)
                pool.wait_ge(idx_step, copied)
                carry_wait(0)
                pool.indirect_dma_start(out=xs, out_offset=None, in_=u2_dram,
                                        in_offset=bass.IndirectOffsetOnAxis(ap=token_now, axis=0),
                                        bounds_check=last_token, oob_is_err=False).then_inc(xs_in, 16)

            def carry_wait(i):
                nc.gpsimd.tensor_tensor(carrier[:, 1 + i:2 + i], carrier[:, 0:1], carrier[:, 0:1], ALU.add).then_inc(idx_step, 1)

            last_token = pool.to_reg(SEQ - 1)
            last_row = pool.to_reg(SEQ * TOPK * CG - 1)
            gather(0, 1)
            passes = pool.value_load(n_passes[0:1, 0:1], min_val=1, max_val=PASSES)
            with pool.Fori(0, passes) as q:
                with pool.Fori(0, NE) as e:
                    n = q * NE + e
                    pool.wait_ge(y_stored, n * (16 * TG))
                    nc.gpsimd.tensor_copy(row_now, row_of[:, :, bass.ds(n, 1)].rearrange("p t o -> p (t o)")).then_inc(idx_step, 1)
                    pool.wait_ge(xs_used, n + 1)
                    gather(n + 1, n * IDX + 4)
                    for t in range(TG):
                        pool.wait_ge(y_made, n * TG + (t + 1))
                        carry_wait(1 + t)
                        pool.indirect_dma_start(out=y_dram, out_offset=bass.IndirectOffsetOnAxis(ap=row_now[:, t:t + 1], axis=0),
                                                in_=y_out[:, t], in_offset=None, bounds_check=last_row,
                                                oob_is_err=False).then_inc(y_stored, 16)
            for i in range(TT):
                pool.wait_ge(squared, CHUNKS + TT + i + 1)
                rstd(P, f_square[:, i:i + 1], f_rstd[:, i:i + 1], D, rstd_made)

        def u2T_part(act, i):
            for f in range(2):
                act.wait_ge(u2_mm, 2 * i + f + 1)
                if i:
                    act.wait_ge(logits_mm, i)
                nc.scalar.activation(u2T[:, 4 * f:4 * f + 4], banks[:, 4 + f].rearrange("p (k t) -> p k t", t=P),
                                     ACT.Copy).then_inc(u2T_made, 1)

        @block.scalar
        def _(act):
            steps = [0]

            def chain(ins):
                steps[0] += 1
                ins.then_inc(act_step, 1)
                act.wait_ge(act_step, steps[0])

            act.dma_start(g_bc, norm_mix_g.to_broadcast([P, D])).then_inc(g_in, 16)
            b2 = b_in[0]
            rows = [(B_A, b2[0:V_OFF], V_OFF // P), (B_SIG, b2[GC_OFF:GC_OFF + D], KT), (B_SIG + KT, b2[O_OFF:O_OFF + D], KT),
                    (B_SIG + 2 * KT, b2[GM_OFF:GM_OFF + D], KT), (LN_G, conv_ln_g[0], KT), (LN_B, conv_ln_b[0], KT),
                    (PW_B, conv_pw_b[0], KT), (MN_G, mlstm_norm_g[0], KT), (DW_B, conv_dw_b[0], KT)]
            for r, src, n in rows:
                act.dma_start(vec_rows[r:r + n], src.rearrange("(r c) -> r c", c=P)).then_inc(vecs_in, 16)
            act.dma_start(tap_rows, conv_dw_w[0]).then_inc(vecs_in, 16)
            with nc.allow_non_contiguous_dma(reason="8 biases"):
                for r, off in ((0, I_OFF), (F_ROW, F_OFF)):
                    act.dma_start(if_bias[r:r + HEADS], b2[off:off + HEADS].rearrange("(r c) -> r c", c=1)).then_inc(vecs_in, 16)
            n_vecs = len(rows) + 3
            act.dma_start(vb_bc, b_in[:, V_OFF:V_OFF + D].to_broadcast([P, D])).then_inc(vb_in, 16)

            def split_hi(n, s):
                act.wait_ge(w_in_sem[s], 16 * (n + 1))
                act.wait_ge(mm_done, pair_tick(n, 8 if s else 2) - PAIR_TICKS)
                nc.scalar.activation(w_hi[:, s], stage[:, s], ACT.Copy).then_inc(w_hi_made[s], 1)

            for i in range(CHUNKS):
                n = P if i < TT else META
                act.wait_ge(x_in[i] if i < TT else meta_in, 16)
                src = x_sb[:, i] if i < TT else meta_sb
                if i:
                    act.wait_ge(squared, i)
                nc.scalar.activation(square_out[0:n], src, ACT.Square, accum_out=square_sum[0:n, i:i + 1]).then_inc(squared, 1)
            act.wait_ge(vecs_transposed, 1)
            nc.scalar.activation(vec, banks[:, 4, 0:VEC_ROWS], ACT.Copy).then_inc(vecs_made, 1)
            act.wait_ge(vecs_transposed, 2)
            nc.scalar.activation(taps, banks[:, 5, 0:KT * CONV_W].rearrange("p (k w) -> p k w", w=CONV_W), ACT.Copy).then_inc(vecs_made, 1)
            act.wait_ge(vecs_made, 1)
            nc.scalar.activation(q_bias, vec[:, B_Q:B_Q + HEADS], ACT.Copy, scale=QK_SCALE).then_inc(vecs_made, 1)
            act.wait_ge(ifw_in, 32)
            nc.scalar.activation(wif_hi, wif, ACT.Copy).then_inc(ifw_hi_made, 1)
            for j in range(2 * TT + 1):
                act.wait_ge(u_transposed, j + 1)
                i, h = j // 2, j % 2
                dst, src = (u_hi[:, 4 * h:4 * h + 4, META + P * i:META + P * (i + 1)], banks[:, j % 4].rearrange("p (k t) -> p k t", t=P)) \
                    if i < TT else (u_hi[:, :, 0:META], banks[:, j % 4, 0:KT * META].rearrange("p (k t) -> p k t", t=META))
                nc.scalar.activation(dst, src, ACT.Copy).then_inc(u_hi_made, 1)
            split_hi(0, 0)
            split_hi(0, 1)
            act.wait_ge(if_mm, 1)
            act.wait_ge(vecs_in, 16 * n_vecs)
            for h in range(2):
                span = slice(HALF * h, HALF * (h + 1))
                nc.scalar.activation(f_row[:, span], banks[F_ROW:F_ROW + HEADS, 6 + h, 0:HALF], ACT.Identity,
                                     bias=if_bias[F_ROW:F_ROW + HEADS]).then_inc(if_rows, 1)
                nc.scalar.activation(i_row[:, span], banks[0:HEADS, 6 + h, 0:HALF], ACT.Identity,
                                     bias=if_bias[0:HEADS]).then_inc(if_rows, 1)
            act.wait_ge(abs_f, 1)
            chain(nc.scalar.activation(e_row, t_row, ACT.Exp, scale=-1.0))
            nc.scalar.activation(t_row, e_row, ACT.Ln, bias=1.0).then_inc(softplus, 1)
            act.wait_ge(m_rows, 1)
            for c in range(CHUNKS):
                a, b = chunk_span(c)
                nc.scalar.activation(gate_rows[W_ROW:W_ROW + HEADS, a:b], gate_rows[0:HEADS, a:b], ACT.Exp,
                                     bias=minus_m_end[:, c:c + 1]).then_inc(gate_rows_made, 1)
                if c:
                    nc.scalar.activation(inter_row[:, a:b], m_row[:, a:b], ACT.Exp, scale=-1.0,
                                         bias=m_prev[:, c:c + 1]).then_inc(gate_rows_made, 1)
            nc.scalar.activation(gate_rows[FLOOR_ROW:FLOOR_ROW + HEADS], b_row, ACT.Exp, scale=-1.0).then_inc(gate_rows_made, 1)

            with act.Fori(0, 4) as j:
                for c in range(GT):
                    act.wait_ge(mm_done, pair_tick(j, 5 + 3 * c))
                    act.wait_ge(glu_out[1 - c], 2 * j + 2 * c)
                    for h in range(2):
                        nc.scalar.activation(sg[:, h], banks[:, 4 * c + 2 + h, 0:HALF], ACT.Sigmoid,
                                             bias=vec[:, bass.ds(2 * j + (KT + c), 1)]).then_inc(glu_sig, 1)
                    if c == 0:
                        split_hi(j + 1, 0)
                split_hi(j + 1, 1)
            for j in range(2):
                n = QK_PAIR + j
                for c in range(GT):
                    act.wait_ge(mm_done, pair_tick(n, 1 + c))
                    hd = 2 * j + c
                    nc.scalar.activation(q_sb[:, hd], banks[:, c], ACT.Identity, bias=q_bias[:, hd:hd + 1],
                                         scale=QK_SCALE).then_inc(qk_out, 1)
                split_hi(n + 1, 0)
                for c in range(GT):
                    act.wait_ge(mm_done, pair_tick(n, 5 + 3 * c))
                    hd = 2 * j + c
                    for h in range(2):
                        nc.scalar.activation(k_sb[:, hd, HALF * h:HALF * (h + 1)], banks[:, 2 + 2 * c + h, 0:HALF], ACT.Identity,
                                             bias=vec[:, B_Q + HEADS + hd:B_Q + HEADS + hd + 1]).then_inc(qk_out, 1)
                split_hi(n + 1, 1)
            for j in range(2):
                split_hi(V_PAIR + j + 1, 0)
                split_hi(V_PAIR + j + 1, 1)

            def sigmoid_pair(j):
                n = SIG_PAIR + j
                for s in range(2):
                    for c in range(GT):
                        act.wait_ge(mm_done, pair_tick(n, (5 + 3 * c) if s else 1 + c))
                        t = 2 * s + c
                        nc.scalar.activation(gates[:, bass.ds(4 * j + t, 1), :], banks[:, 4 + t:5 + t], ACT.Sigmoid,
                                             bias=vec[:, bass.ds(4 * j + (B_SIG + t), 1)]).then_inc(sig_out[t], 1)
                    split_hi(n + 1, s)

            with act.Fori(0, 4) as j:
                sigmoid_pair(j)
            act.wait_ge(conv_step, CONV_W * KT)
            with act.Fori(4, 6) as j:
                sigmoid_pair(j)

            for k in range(KT):
                act.wait_ge(centered, k + 1)
                nc.scalar.activation(squares[:, k], conv[:, k], ACT.Square).then_inc(squares_made, 1)
            act.wait_ge(cols_mm, 1)
            nc.scalar.activation(cols, banks[:, 1, 0:CHUNKS * ROWS].rearrange("p (c r) -> p c r", r=ROWS), ACT.Copy).then_inc(cols_made, 1)
            for h in range(HEADS):
                act.wait_ge(e_made, TT * (h + 1))
                nc.scalar.activation(probs[:, h], probs[:, h], ACT.Exp, scale=-1.0).then_inc(d_made, 1)
            act.wait_ge(ln_mm, 2)
            nc.scalar.activation(squares[:, KT - 1], banks[:, 0], ACT.Copy).then_inc(var_made, 1)

            def scaled_keys(c):
                n = P if c else META
                act.wait_ge(kt_mm, c + 1)
                act.wait_ge(outer_mm, HEADS * c)
                for h in range(HEADS):
                    nc.scalar.activation(kw_sb[0:n, h], banks[0:n, 1, P * h:P * (h + 1)], ACT.Copy,
                                         scale=cols[0:n, c, W_ROW + h:W_ROW + h + 1]).then_inc(kw_made, 1)

            scaled_keys(0)
            for i in range(TT):
                act.wait_ge(den_made, i + 1)
                act.wait_ge(ht_mm, 2 * i)
                for h in range(HEADS):
                    nc.scalar.activation(h_tok[:, h], banks[:, 4 + h, 0:DV], ACT.Square, scale=den_inv[:, h:h + 1],
                                         accum_out=head_square[:, h:h + 1]).then_inc(h_squared, 1)
                if i + 1 < TT:
                    scaled_keys(i + 1)
                act.wait_ge(h_scaled, i + 1)
                act.wait_ge(h_squared, HEADS * (i + 1))
                for h in range(HEADS):
                    nc.scalar.activation(h_tok[:, h], banks[:, 4 + h, 0:DV], ACT.Copy,
                                         scale=head_scale[:, h:h + 1]).then_inc(tok_made, 1)
                for f in range(2):
                    act.wait_ge(ht_gated, 2 * i + f + 1)
                    nc.scalar.activation(h_hi[:, 4 * f:4 * f + 4, P * i:P * (i + 1)],
                                         gates[:, OG + 4 * f:OG + 4 * f + 4, P * i:P * (i + 1)], ACT.Copy).then_inc(h_hi_made, 1)
            for k in range(KT):
                act.wait_ge(normed, k + 1)
                nc.scalar.activation(conv[:, k], conv[:, k], ACT.Silu, scale=vec[:, LN_G + k:LN_G + k + 1],
                                     bias=vec[:, LN_B + k:LN_B + k + 1]).then_inc(silu_made, 1)
            for k in range(KT):
                act.wait_ge(silu_made, k + 1)
                nc.scalar.activation(silu_hi[:, k], conv[:, k], ACT.Copy).then_inc(silu_hi_made, 1)
            for n in range(PW_PAIR, OW_PAIR + 1):
                for s in range(2):
                    split_hi(n + 1, s)
            for j in range(2):
                for t in range(4):
                    act.wait_ge(mixed, 4 * j + t + 1)
                    nc.scalar.activation(mix_hi[:, 4 * j + t], gates[:, GC + 4 * j + t], ACT.Copy).then_inc(mix_hi_made, 1)
                for s in range(2):
                    split_hi(OW_PAIR + 2 + j, s)

            for s in range(2):
                act.wait_ge(w_lo_made[s], WO_PAIR + 2)
            for i in range(TT):
                act.wait_ge(wo_out, TT + i + 1)
                if i >= 2:
                    act.wait_ge(u2_stored[i - 2], 16)
                    act.wait_ge(u2_mm, 2 * (i - 1))
                nc.scalar.activation(u2[:, i % 2], h_res[:, i], ACT.Square, accum_out=h_square[:, i:i + 1]).then_inc(squared, 1)
                if i:
                    u2T_part(act, i - 1)
            u2T_part(act, TT - 1)
            act.wait_ge(shifted, 1)
            nc.scalar.activation(gate_w, gate_w, ACT.Exp).then_inc(gate_exp, 1)

            act.wait_ge(mm_done, pair_tick(WO_PAIR + 1, 8))
            for m in range(2):
                act.wait_ge(xs_used, 1)
                nc.scalar.activation(xT[:, 4 * m:4 * m + 4], banks[:, m, 0:4 * SLOTS].rearrange("p (k s) -> p k s", s=SLOTS),
                                     ACT.Copy).then_inc(xT_made, 1)
            act.wait_ge(passes_made, 1)
            passes = act.value_load(n_passes[0:1, 0:1], min_val=1, max_val=PASSES)
            with act.Fori(0, passes) as q:
                with act.Fori(0, NE) as e:
                    n = q * NE + e
                    act.wait_ge(glu_made, n * TG)
                    for g in range(CG):
                        act.dma_start(bias1[32 * g:32 * (g + 1)],
                                      expert_b1[0, bass.ds(e, 1), :].rearrange("e (h j n) -> e j h n", h=2, j=CG)[:, g]
                                      .to_broadcast([32, 2, GRP])).then_inc(b1_in, 16)
                    act.wait_ge(y_made, n * TG)
                    for g in range(CG):
                        act.dma_start(bias2[32 * g:32 * (g + 1)], expert_b2[0, bass.ds(e, 1), GRP * g:GRP * (g + 1)]
                                      .to_broadcast([32, GRP])).then_inc(b2_in, 16)

                    def sigmoid(t):
                        act.wait_ge(glu_made, n * TG + (t + 1))
                        nc.scalar.activation(sig[:, t], hid[:, t, 0:GRP], ACT.Sigmoid, scale=ALPHA).then_inc(sig_made, 1)

                    def take_actT(t):
                        act.wait_ge(act_mm, n * TG + (t + 1))
                        nc.scalar.activation(actT.rearrange("p (j h) s -> p h j s", h=2)[:, :, :, 32 * t:32 * (t + 1)],
                                             banks[:, 6 + t % 2, 0:2 * P].rearrange("p (h j s) -> p h j s", h=2, j=CG),
                                             ACT.Copy).then_inc(actT_made, 1)

                    sigmoid(0)
                    sigmoid(1)
                    take_actT(0)
                    sigmoid(2)
                    take_actT(1)
                    act.wait_ge(xs_used, n + 2)
                    for m in range(2):
                        nc.scalar.activation(xT[:, 4 * m:4 * m + 4], banks[:, m, 0:4 * SLOTS].rearrange("p (k s) -> p k s", s=SLOTS),
                                             ACT.Copy).then_inc(xT_made, 1)
                    take_actT(2)
            for i in range(TT):
                act.wait_ge(summed, i + 1)
                nc.scalar.activation(y_in[:, i, 0], h_res[:, i], ACT.Square, accum_out=f_square[:, i:i + 1]).then_inc(squared, 1)

        @block.tensor
        def _(pe):
            def product(dst, stationary, moving, k, ks=KT, tick=None):
                a, b = stationary
                c, d = moving
                for n, (l, r) in enumerate(((a, c), (b, c), (a, d))):
                    last = nc.tensor.matmul(dst, l, r, start=(k == 0 and n == 0), stop=(k == ks - 1 and n == 2))
                return last

            def weights(s, k, c):
                return w_hi[:, s, k, P * c:P * (c + 1)], w_lo[:, s, k, P * c:P * (c + 1)]

            def channel_tile(s, c, src, dst, span, ticks=None):
                hi, lo = src
                for k in range(KT):
                    last = product(dst, weights(s, k, c), (hi[:, k, span], lo[:, k, span]), k)
                if ticks:
                    last.then_inc(mm_done, ticks)

            u = (u_hi, u_lo)
            halves = [slice(HALF * h, HALF * (h + 1)) for h in range(2)]
            main = slice(META, NT)

            pe.wait_ge(consts_made, 1)
            pe.wait_ge(vecs_in, 16 * 12)
            nc.tensor.transpose(banks[:, 4, 0:VEC_ROWS], vec_rows, ident[0:VEC_ROWS, 0:VEC_ROWS]).then_inc(vecs_transposed, 1)
            for k in range(KT):
                last = nc.tensor.transpose(banks[:, 5, CONV_W * k:CONV_W * (k + 1)], tap_rows[:, P * k:P * (k + 1)],
                                           ident[0:CONV_W, 0:CONV_W])
            last.then_inc(vecs_transposed, 1)
            for j in range(2 * TT + 1):
                i, h = j // 2, j % 2
                pe.wait_ge(scaled, i + 1)
                if j >= 4:
                    pe.wait_ge(u_lo_made, j - 3)
                if i < TT:
                    for k in range(4):
                        col = P * (4 * h + k)
                        last = nc.tensor.transpose(banks[:, j % 4, P * k:P * (k + 1)], x_sb[:, i, col:col + P], ident)
                else:
                    for k in range(KT):
                        last = nc.tensor.transpose(banks[:, j % 4, META * k:META * (k + 1)], meta_sb[:, P * k:P * (k + 1)],
                                                   ident[0:META, 0:META])
                last.then_inc(u_transposed, 1)
            pe.wait_ge(u_lo_made, 2 * TT + 1)
            pe.wait_ge(ifw_lo_made, 1)
            for h in range(2):
                for k in range(KT):
                    last = product(banks[:, 6 + h, 0:HALF], (wif_hi[:, k], wif_lo[:, k]),
                                   (u_hi[:, k, halves[h]], u_lo[:, k, halves[h]]), k)
            last.then_inc(if_mm, 1)

            def wait_weights(n, s):
                pe.wait_ge(w_lo_made[s], n + 1)

            pe.wait_ge(if_rows, 4)
            pe.wait_ge(vecs_made, 2)
            with pe.Fori(0, 4) as j:
                for s in range(2):
                    wait_weights(j, s)
                    for c in range(GT):
                        pe.wait_ge(glu_out[c], 2 * j)
                        for h in range(2):
                            channel_tile(s, c, u, banks[:, 4 * c + 2 * s + h, 0:HALF], halves[h],
                                         (3 if s else 1) if h else None)
            for j in range(2):
                for s in range(2):
                    wait_weights(QK_PAIR + j, s)
                    for c in range(GT):
                        pe.wait_ge(glu_out[0], 8)
                        pe.wait_ge(glu_out[1], 8)
                        if s == 0:
                            if j:
                                pe.wait_ge(qk_out, 1 + c)
                            channel_tile(0, c, u, banks[:, c], main, 1)
                        else:
                            if j:
                                pe.wait_ge(qk_out, 4 + 2 * c)
                            for h in range(2):
                                channel_tile(1, c, u, banks[:, 2 + 2 * c + h, 0:HALF], halves[h], 3 if h else None)

            def token_tile(s, src, dst, span, ticks=None):
                hi, lo = src
                for k in range(KT):
                    last = product(dst, (hi[:, k, span], lo[:, k, span]), (w_hi[:, s, k], w_lo[:, s, k]), k)
                if ticks:
                    last.then_inc(mm_done, ticks)

            pe.wait_ge(qk_out, 12)
            for j in range(2):
                for s in range(2):
                    wait_weights(V_PAIR + j, s)
                    for i in range(TT + 1):
                        if j and s == 0:
                            pe.wait_ge(v_out, i + 1)
                        span = slice(META + P * i, META + P * (i + 1)) if i < TT else slice(0, P)
                        token_tile(s, u, banks[:, i, GRP * s:GRP * (s + 1)], span,
                                   (2 if i == TT else 1) if s else (2 if i == TT else None))
            pe.wait_ge(v_out, 2 * (TT + 1))

            with pe.Fori(0, 6) as j:
                for s in range(2):
                    wait_weights(j + SIG_PAIR, s)
                    for c in range(GT):
                        t = 2 * s + c
                        pe.wait_ge(sig_out[t], j)
                        channel_tile(s, c, u, banks[:, 4 + t], main, 3 if s else 1)

            def column_means(src):
                for k in range(KT):
                    last = nc.tensor.matmul(banks[:, 0], mean_w, src[:, k], start=k == 0, stop=k == KT - 1)
                last.then_inc(ln_mm, 1)

            pe.wait_ge(conv_step, CONV_W * KT)
            column_means(conv)
            pe.wait_ge(gate_rows_made, 2 * CHUNKS)
            for c in range(CHUNKS):
                a = chunk_span(c)[0]
                last = nc.tensor.transpose(banks[:, 1, ROWS * c:ROWS * (c + 1)], gate_rows[0:ROWS, a:a + P], ident[0:ROWS, 0:ROWS])
            last.then_inc(cols_mm, 1)
            for t in range(4):
                pe.wait_ge(sig_out[t], 6)
            for h in range(HEADS):
                if h >= 2:
                    pe.wait_ge(head_out, h - 1)
                sel = ident[0:HEADS, h:h + 1].to_broadcast([HEADS, P])
                nc.tensor.matmul(banks[:, 2 + h % 2], sel, m_row[:, main], start=True, stop=True)
                nc.tensor.matmul(banks[:, 4 + h % 2], sel, inter_row[:, main], start=True, stop=True)
                for i in range(TT):
                    last = nc.tensor.matmul(banks[:, 6 + h % 2, P * i:P * (i + 1)], k_sb[:, h, META + P * i:META + P * (i + 1)],
                                            q_sb[:, h, P * i:P * (i + 1)], start=True, stop=True)
                last.then_inc(head_mm, 1)
            pe.wait_ge(squares_made, KT)
            column_means(squares)

            def state_part(c):
                if c:
                    pe.wait_ge(ht_gated, 2 * (c - 1))
                pe.wait_ge(cols_made, 1)
                pe.wait_ge(kw_made, HEADS * c)
                a = chunk_span(c)[0]
                for h in range(HEADS):
                    last = nc.tensor.transpose(banks[:, 1, P * h:P * (h + 1)], k_sb[:, h, a:a + P], ident)
                last.then_inc(kt_mm, 1)
                n = P if c else META
                for h in range(HEADS):
                    pe.wait_ge(kw_made, HEADS * c + h + 1)
                    if c or h >= 2:
                        pe.wait_ge(state_out, HEADS * c + h - 1)
                    else:
                        pe.wait_ge(head_out, HEADS)
                    nc.tensor.matmul(banks[:, 2 + h % 2, 0:VW], kw_sb[0:n, h], v_sb[:, c - 1, h] if c else v_meta[:, h],
                                     start=True, stop=True).then_inc(outer_mm, 1)

            state_part(0)
            for i in range(TT):
                pe.wait_ge(head_out, HEADS)
                pe.wait_ge(tok_made, HEADS * i)
                for h in range(HEADS):
                    nc.tensor.matmul(banks[:, 4 + h, 0:VW], probs[:, h, P * i:P * (i + 1)], v_sb[:, i, h], start=True, stop=False)
                    pe.wait_ge(state_out, HEADS * i + h + 1)
                    nc.tensor.matmul(banks[:, 4 + h, 0:VW], q_sb[:, h, P * i:P * (i + 1)], state[:, h],
                                     start=False, stop=True).then_inc(h_mm, 1)
                if i + 1 < TT:
                    state_part(i + 1)
                pe.wait_ge(tok_made, HEADS * (i + 1))
                if i == 0:
                    pe.wait_ge(var_made, 1)
                for f in range(2):
                    if f == 1 and i + 1 < TT:
                        pe.wait_ge(kw_made, HEADS * (i + 2))
                    if i:
                        pe.wait_ge(ht_gated, 2 * i)
                    for d in range(4):
                        hd, part = (4 * f + d) // 2, d % 2
                        last = nc.tensor.transpose(banks[:, f, P * d:P * (d + 1)], h_tok[:, hd, P * part:P * (part + 1)], ident)
                    last.then_inc(ht_mm, 1)

            whole = slice(0, SEQ)
            pe.wait_ge(silu_lo_made, KT)
            for j in range(2):
                for s in range(2):
                    wait_weights(PW_PAIR + j, s)
                    for c in range(GT):
                        if j:
                            pe.wait_ge(pw_out, 2 * s + c + 1)
                        channel_tile(s, c, (silu_hi, silu_lo), banks[:, 4 + 2 * s + c], whole, 3 if s else 1)
            pe.wait_ge(h_lo_made, 2 * TT)
            for j in range(2):
                for s in range(2):
                    wait_weights(OW_PAIR + j, s)
                    for c in range(GT):
                        if j:
                            pe.wait_ge(ow_out, 2 * s + c + 1)
                        channel_tile(s, c, (h_hi, h_lo), banks[:, 2 * s + c], whole, 3 if s else 1)
            pe.wait_ge(mix_lo_made, KT)
            pe.wait_ge(pw_out, KT)
            pe.wait_ge(ow_out, KT)
            for j in range(2):
                for s in range(2):
                    wait_weights(WO_PAIR + j, s)
                    for i in range(TT):
                        token_tile(s, (mix_hi, mix_lo), banks[:, 4 * (1 - j) + i, GRP * s:GRP * (s + 1)],
                                   slice(P * i, P * (i + 1)), (3 if i == TT - 1 else 1) if s else (2 if i == TT - 1 else None))

            pe.wait_ge(router_in, 32)
            pe.wait_ge(wo_out, TT)
            for i in range(TT):
                pe.wait_ge(u2_made, i + 1)
                for f in range(2):
                    if i:
                        pe.wait_ge(u2T_made, 2 * (i - 1) + f + 1)
                    for k in range(4):
                        col = P * (4 * f + k)
                        last = nc.tensor.transpose(banks[:, 4 + f, P * k:P * (k + 1)], u2[:, i % 2, col:col + P], ident)
                    last.then_inc(u2_mm, 1)
                pe.wait_ge(u2T_made, 2 * (i + 1))
                if i >= 2:
                    pe.wait_ge(routed, i - 1)
                for k in range(KT):
                    last = nc.tensor.matmul(banks[:, 6 + i % 2, 0:NE], u2T[:, k], w_router[:, k], start=k == 0, stop=k == KT - 1)
                last.then_inc(logits_mm, 1)
            pe.wait_ge(moe_consts, 2)
            pe.wait_ge(mask_made, 1)
            for i in range(TT + 1):
                for m in range(min(i + 1, TT)):
                    last = nc.tensor.matmul(banks[:, 7, NE * i:NE * (i + 1)], earlier if m == i else all_ones, mask[:, m],
                                            start=m == 0, stop=m == min(i, TT - 1))
            last.then_inc(place_mm, 1)

            def x_transposes(n):
                pe.wait_ge(xs_in, (n + 1) * 16)
                for k in range(KT):
                    last = nc.tensor.transpose(banks[:, k // 4, SLOTS * (k % 4):SLOTS * (k % 4 + 1)], xs[:, P * k:P * (k + 1)],
                                               ident[0:SLOTS, 0:SLOTS])
                last.then_inc(xs_used, 1)

            pe.wait_ge(wo_out, 2 * TT)
            x_transposes(0)
            pe.wait_ge(passes_made, 1)
            passes = pe.value_load(n_passes[0:1, 0:1], min_val=1, max_val=PASSES)
            with pe.Fori(0, passes) as q:
                with pe.Fori(0, NE) as e:
                    n = q * NE + e

                    def hidden(k, t):
                        for g in range(CG):
                            last = nc.tensor.matmul(banks[32 * g:32 * (g + 1), t].rearrange("p (h n) -> p h n", h=2),
                                                    xT[:, k, 32 * t:32 * (t + 1)], w1_ring[k][:, :, GRP * g:GRP * (g + 1)],
                                                    start=k == 0, stop=k == KT - 1, tile_position=(0, 32 * g))
                        return last

                    pe.wait_ge(xT_made, (n + 1) * 2)
                    pe.wait_ge(act_made, n * TG)
                    for k in range(KT - 2):
                        pe.wait_ge(ring_in[k], (n + 1) * 16)
                        for t in range(TG):
                            last = hidden(k, t)
                        last.then_inc(ring_used[k], 1)
                    for k in (KT - 2, KT - 1):
                        pe.wait_ge(ring_in[k], (n + 1) * 16)
                    for t in range(TG):
                        last = hidden(KT - 2, t)
                        if t == TG - 1:
                            last.then_inc(ring_used[KT - 2], 1)
                        hidden(KT - 1, t).then_inc(hid_mm, 1)

                    def transposes(t):
                        pe.wait_ge(act_made, n * TG + (t + 1))
                        if t >= 2:
                            pe.wait_ge(actT_made, n * TG + (t - 1))
                        for h in range(2):
                            last = nc.tensor.transpose(banks[:, 6 + t % 2, P * h:P * (h + 1)], act_v[:, t, P * h:P * (h + 1)], ident)
                        last.then_inc(act_mm, 1)

                    def second(t):
                        pe.wait_ge(actT_made, n * TG + (t + 1))
                        pe.wait_ge(y_made, n * TG)
                        for k in range(KT):
                            if t == 0 and k % 2 == 0:
                                pe.wait_ge(ring_in[W1C + k // 2], (n + 1) * 16)
                            for g in range(CG):
                                last = nc.tensor.matmul(banks[32 * g:32 * (g + 1), 3 + t, 0:GRP], actT[:, k, 32 * t:32 * (t + 1)],
                                                        w2_ring[k // 2][:, k % 2, GRP * g:GRP * (g + 1)],
                                                        start=k == 0, stop=k == KT - 1, tile_position=(0, 32 * g))
                            if t == TG - 1 and k % 2 == 1 and k < KT - 1:
                                last.then_inc(ring_used[W1C + k // 2], 1)
                        last.then_inc(y_mm, 1)

                    transposes(0)
                    second(0)
                    transposes(1)
                    second(1)
                    transposes(2)
                    x_transposes(n + 1)
                    second(2)

        def scale_out(dve, i):
            if i == 0:
                dve.wait_ge(last_g_in, 16)
            dve.wait_ge(rstd_made, CHUNKS + TT + i + 1)
            nc.vector.scalar_tensor_tensor(out=h_res[:, i], in0=h_res[:, i], scalar=f_rstd[:, i:i + 1], in1=last_g,
                                           op0=ALU.mult, op1=ALU.mult).then_inc(out_made, 1)

        @block.vector
        def _(dve):
            steps = [0]

            def chain(ins):
                steps[0] += 1
                ins.then_inc(dve_step, 1)
                dve.wait_ge(dve_step, steps[0])

            dve.wait_ge(g_in, 16)
            for i in range(CHUNKS):
                dve.wait_ge(rstd_made, i + 1)
                rows, n = (x_sb[:, i], P) if i < TT else (meta_sb, META)
                nc.vector.scalar_tensor_tensor(out=rows, in0=rows, scalar=row_rstd[0:n, i:i + 1], in1=g_bc[0:n],
                                               op0=ALU.mult, op1=ALU.mult).then_inc(scaled, 1)
            for j in range(2 * TT + 1):
                dve.wait_ge(u_hi_made, j + 1)
                i, h = j // 2, j % 2
                if i < TT:
                    span = (slice(None), slice(4 * h, 4 * h + 4), slice(META + P * i, META + P * (i + 1)))
                    src = banks[:, j % 4].rearrange("p (k t) -> p k t", t=P)
                else:
                    span = (slice(None), slice(None), slice(0, META))
                    src = banks[:, j % 4, 0:KT * META].rearrange("p (k t) -> p k t", t=META)
                nc.vector.tensor_tensor(u_lo[span], src, u_hi[span].bitcast(F32), ALU.subtract).then_inc(u_lo_made, 1)

            dve.wait_ge(consts_made, 6)
            for c in range(CHUNKS):
                a = chunk_span(c)[0]
                chain(nc.vector.memset(keep_row[:, a:a + 1], 0.0))
            dve.wait_ge(if_rows, 4)
            nc.vector.scalar_tensor_tensor(out=t_row, in0=f_row, scalar=-1.0, in1=f_row, op0=ALU.mult, op1=ALU.max).then_inc(abs_f, 1)
            dve.wait_ge(softplus, 1)
            chain(nc.vector.scalar_tensor_tensor(out=f_row, in0=f_row, scalar=0.0, in1=t_row, op0=ALU.min, op1=ALU.subtract))
            chain(nc.vector.tensor_tensor_scan(b_row, keep_row, f_row, 0.0, ALU.mult, ALU.add))
            chain(nc.vector.tensor_tensor(gate_rows[0:HEADS], i_row, b_row, ALU.subtract))
            chain(nc.vector.memset(m_prev[:, 0:1], 0.0))
            for c in range(CHUNKS):
                a, b = chunk_span(c)
                ar = gate_rows[0:HEADS, a:b]
                chain(nc.vector.tensor_tensor_scan(m_row[:, a:b], ar, ar, m_prev[:, c:c + 1], ALU.max, ALU.max))
                if c + 1 < CHUNKS:
                    chain(nc.vector.tensor_tensor(m_prev[:, c + 1:c + 2], b_row[:, b - 1:b], m_row[:, b - 1:b], ALU.add))
            chain(nc.vector.tensor_scalar(minus_m_end, m_row[:, META - 1::P], -1.0, None, ALU.mult))
            nc.vector.tensor_tensor(b_row, b_row, m_row, ALU.add).then_inc(m_rows, 1)

            def conv_tile(ct):
                src, dst = conv_in[:, bass.ds(ct, 1), :], conv[:, bass.ds(ct, 1), :]
                nc.vector.tensor_scalar(dst, src[:, :, 0:SEQ], taps[:, bass.ds(ct, 1), 0], vec[:, bass.ds(ct + DW_B, 1)],
                                        ALU.mult, ALU.add).then_inc(conv_step, 1)
                for w in range(1, CONV_W):
                    dve.wait_ge(conv_step, ct * CONV_W + w)
                    nc.vector.scalar_tensor_tensor(out=dst, in0=src[:, :, w:w + SEQ], scalar=taps[:, bass.ds(ct, 1), w], in1=dst,
                                                   op0=ALU.mult, op1=ALU.add).then_inc(conv_step, 1)

            dve.wait_ge(vecs_made, 3)
            with dve.Fori(0, 4) as j:
                for c in range(GT):
                    for h in range(2):
                        dve.wait_ge(glu_sig, 4 * j + (2 * c + h + 1))
                        nc.vector.scalar_tensor_tensor(
                            out=conv_in[:, bass.ds(2 * j + c, 1), PADL + HALF * h:PADL + HALF * (h + 1)],
                            in0=banks[:, 4 * c + h:4 * c + h + 1, 0:HALF], scalar=vec[:, bass.ds(2 * j + c, 1)], in1=sg[:, h:h + 1],
                            op0=ALU.add, op1=ALU.mult).then_inc(glu_out[c], 1)
                dve.wait_ge(glu_out[0], 2 * j + 2)
                conv_tile(j)

            def take_v(j):
                if j == 0:
                    dve.wait_ge(vb_in, 16)
                for i in range(TT + 1):
                    dve.wait_ge(mm_done, pair_tick(V_PAIR + j, 3 + i + (i == TT)))
                    n, dst = (P, v_sb[:, i]) if i < TT else (META, v_meta)
                    nc.vector.tensor_tensor(dst[:, 2 * j:2 * j + 2, 0:DV], banks[0:n, i].rearrange("p (h v) -> p h v", v=DV),
                                            vb_bc[0:n, 512 * j:512 * (j + 1)].rearrange("p (h v) -> p h v", v=DV),
                                            ALU.add).then_inc(v_out, 1)

            dve.wait_ge(glu_out[1], 8)
            with dve.Fori(4, 6) as ct:
                conv_tile(ct)
            chain(nc.vector.memset(v_sb[:, :, :, DV:VW], 1.0))
            chain(nc.vector.memset(v_meta[:, :, DV:VW], 1.0))
            take_v(0)
            conv_tile(6)
            take_v(1)
            conv_tile(7)

            dve.wait_ge(ln_mm, 1)
            for k in range(KT):
                nc.vector.tensor_tensor(conv[:, k], conv[:, k], banks[:, 0], ALU.subtract).then_inc(centered, 1)
            dve.wait_ge(cols_made, 1)
            for h in range(HEADS):
                dve.wait_ge(head_mm, h + 1)
                for i in range(TT):
                    nc.vector.scalar_tensor_tensor(out=probs[:, h, P * i:P * (i + 1)], in0=banks[:, 2 + h % 2, P * i:P * (i + 1)],
                                                   scalar=cols[:, i + 1, h:h + 1], in1=maskpos, op0=ALU.subtract,
                                                   op1=ALU.max).then_inc(e_made, 1)
                nc.vector.tensor_copy(decay[:, h], banks[:, 4 + h % 2, P - 1::P])
                nc.vector.tensor_tensor(q_sb[:, h], q_sb[:, h], banks[:, 4 + h % 2], ALU.mult)
                dve.wait_ge(d_made, h + 1)
                nc.vector.tensor_tensor(probs[:, h], probs[:, h], banks[:, 6 + h % 2], ALU.mult).then_inc(head_out, 1)

            def update_state(c):
                for h in range(HEADS):
                    dve.wait_ge(outer_mm, HEADS * c + h + 1)
                    src = banks[:, 2 + h % 2, 0:VW]
                    if c == 0:
                        nc.vector.tensor_copy(state[:, h], src).then_inc(state_out, 1)
                    else:
                        dve.wait_ge(h_mm, HEADS * (c - 1) + h + 1)
                        nc.vector.scalar_tensor_tensor(out=state[:, h], in0=state[:, h], scalar=decay[:, h, c - 1:c], in1=src,
                                                       op0=ALU.mult, op1=ALU.add).then_inc(state_out, 1)

            update_state(0)
            for i in range(TT):
                dve.wait_ge(h_mm, HEADS * (i + 1))
                dve.wait_ge(h_squared, HEADS * i)
                dve.wait_ge(h_scaled, i)
                den = banks[:, 4:8, DV:VW].rearrange("p h v -> p (h v)")
                chain(nc.vector.scalar_tensor_tensor(out=den_inv, in0=den, scalar=-1.0, in1=cols[:, i + 1, FLOOR_ROW:FLOOR_ROW + HEADS],
                                                     op0=ALU.mult, op1=ALU.max))
                chain(nc.vector.tensor_tensor(den_inv, den_inv, den, ALU.max))
                nc.vector.reciprocal(den_inv, den_inv).then_inc(den_made, 1)
                if i + 1 < TT:
                    update_state(i + 1)
                for f in range(2):
                    dve.wait_ge(ht_mm, 2 * i + f + 1)
                    dve.wait_ge(og_made, KT)
                    og = gates[:, OG + 4 * f:OG + 4 * f + 4, P * i:P * (i + 1)]
                    nc.vector.tensor_tensor(og, og, banks[:, f].rearrange("p (d t) -> p d t", t=P), ALU.mult).then_inc(ht_gated, 1)
                for f in range(2):
                    dve.wait_ge(h_hi_made, 2 * i + f + 1)
                    span = (slice(None), slice(4 * f, 4 * f + 4), slice(P * i, P * (i + 1)))
                    nc.vector.tensor_tensor(h_lo[span], gates[:, OG:OG + KT][span], h_hi[span].bitcast(F32),
                                            ALU.subtract).then_inc(h_lo_made, 1)
            dve.wait_ge(rstd_bc_made, 1)
            dve.wait_ge(centered, KT)
            for k in range(KT):
                nc.vector.tensor_tensor(conv[:, k], conv[:, k], squares[:, KT - 1], ALU.mult).then_inc(normed, 1)
            for k in range(KT):
                dve.wait_ge(silu_hi_made, k + 1)
                nc.vector.tensor_tensor(silu_lo[:, k], conv[:, k], silu_hi[:, k].bitcast(F32), ALU.subtract).then_inc(silu_lo_made, 1)
            for j in range(2):
                for t in range(4):
                    dve.wait_ge(mm_done, pair_tick(PW_PAIR + j, (1 + t) if t < 2 else 3 * t - 1))
                    g = gates[:, GC + 4 * j + t]
                    nc.vector.scalar_tensor_tensor(out=g, in0=banks[:, 4 + t], scalar=vec[:, PW_B + 4 * j + t:PW_B + 4 * j + t + 1],
                                                   in1=g, op0=ALU.add, op1=ALU.mult).then_inc(pw_out, 1)
            for j in range(2):
                for t in range(4):
                    n = 4 * j + t
                    dve.wait_ge(mm_done, pair_tick(OW_PAIR + j, (1 + t) if t < 2 else 3 * t - 1))
                    g, m = gates[:, GC + n], gates[:, GM + n]
                    nc.vector.tensor_tensor(m, m, banks[:, t], ALU.mult).then_inc(ow_out, 1)
                    dve.wait_ge(ow_out, n + 1)
                    nc.vector.tensor_tensor(g, g, m, ALU.add).then_inc(mixed, 1)
                    dve.wait_ge(mix_hi_made, n + 1)
                    nc.vector.tensor_tensor(mix_lo[:, n], g, mix_hi[:, n].bitcast(F32), ALU.subtract).then_inc(mix_lo_made, 1)
            dve.wait_ge(res_in, 16)
            for j in range(2):
                for i in range(TT):
                    dve.wait_ge(mm_done, pair_tick(WO_PAIR + j, 3 + i if i < TT - 1 else 8))
                    r = h_res[:, i, 512 * j:512 * (j + 1)]
                    nc.vector.tensor_tensor(r, r, banks[:, 4 * (1 - j) + i], ALU.add).then_inc(wo_out, 1)

            dve.wait_ge(gf_in, 16)
            for i in range(TT):
                dve.wait_ge(rstd_made, CHUNKS + i + 1)
                nc.vector.scalar_tensor_tensor(out=u2[:, i % 2], in0=h_res[:, i], scalar=h_rstd[:, i:i + 1], in1=gf_bc,
                                               op0=ALU.mult, op1=ALU.mult).then_inc(u2_made, 1)
            dve.wait_ge(router_in, 32)
            for i in range(TT):
                dve.wait_ge(logits_mm, i + 1)
                nc.vector.tensor_tensor(logits[:, i], banks[:, 6 + i % 2, 0:NE], rb_bc, ALU.add).then_inc(routed, 1)
                dve.wait_ge(routed, i + 1)
                chain(nc.vector.max(top[:, i], logits[:, i]))
                chain(nc.vector.max_index(top_idx[:, i], top[:, i], logits[:, i]))
            chain(nc.vector.tensor_copy(expert_f, top_idx[:, :, 0:TOPK]))
            dve.wait_ge(moe_consts, 2)
            TK = TT * TOPK
            chosen = expert_f.rearrange("p i k -> p (i k)")
            chain(nc.vector.tensor_tensor(one_hot, expert_id.unsqueeze(1).to_broadcast([P, TK, NE]),
                                          chosen.unsqueeze(2).to_broadcast([P, TK, NE]), ALU.is_equal))
            with nc.allow_low_precision(reason="ones and zeros"):
                nc.vector.tensor_reduce(mask, one_hot.rearrange("p (i k) e -> p i e k", k=TOPK), axis=AX.X, op=ALU.add).then_inc(mask_made, 1)
            nc.vector.tensor_tensor(gate_w, top[:, :, 0:TOPK], top[:, :, 0:1].to_broadcast([P, TT, TOPK]), ALU.subtract).then_inc(shifted, 1)
            dve.wait_ge(place_mm, 1)
            chain(nc.vector.tensor_tensor(picked.rearrange("p (i k) e -> p i k e", k=TOPK), one_hot.rearrange("p (i k) e -> p i k e", k=TOPK),
                                          banks[:, 7, 0:TT * NE].rearrange("p (i e) -> p i e", e=NE).unsqueeze(2).to_broadcast([P, TT, TOPK, NE]),
                                          ALU.mult))
            chain(nc.vector.tensor_reduce(place, picked, axis=AX.X, op=ALU.add))
            nc.vector.scalar_tensor_tensor(out=dest, in0=place, scalar=float(NE), in1=chosen, op0=ALU.mult, op1=ALU.add).then_inc(dest_made, 1)
            chain(nc.vector.reduce_max(count_max, banks[:, 7, TT * NE:(TT + 1) * NE], axis=AX.X))
            chain(nc.vector.tensor_scalar(over[:, 0:PASSES - 1], steps96, count_max, None, ALU.is_lt))
            chain(nc.vector.tensor_reduce(count_max, over[:, 0:PASSES - 1], axis=AX.X, op=ALU.add))
            nc.vector.tensor_scalar(n_passes, count_max, 1.0, None, ALU.add).then_inc(passes_made, 1)
            dve.wait_ge(gate_exp, 1)
            chain(nc.vector.tensor_reduce(gate_sum, gate_w, axis=AX.X, op=ALU.add))
            chain(nc.vector.reciprocal(gate_sum, gate_sum))
            chain(nc.vector.tensor_tensor(gate_w, gate_w, gate_sum.unsqueeze(2).to_broadcast([P, TT, TOPK]), ALU.mult))
            dve.wait_ge(table_in, 16 * (1 + CG * TG))
            nc.vector.tensor_scalar(token_of, token_of, 2, None, ALU.arith_shift_right).then_inc(tables_made, 1)
            nc.vector.tensor_scalar(row_of, row_of, float(CG), group_of, ALU.mult, ALU.add).then_inc(tables_made, 1)

            passes = dve.value_load(n_passes[0:1, 0:1], min_val=1, max_val=PASSES)
            STEPS = 3 * TG
            with dve.Fori(0, passes) as q:
                with dve.Fori(0, NE) as e:
                    n = q * NE + e
                    k = [0]

                    def own(ins):
                        k[0] += 1
                        ins.then_inc(ffn_step, 1)
                        dve.wait_ge(ffn_step, n * STEPS + k[0])

                    def clamped(t):
                        dve.wait_ge(hid_mm, n * TG + (t + 1))
                        own(nc.vector.tensor_tensor(hid[:, t], banks[:, t], bias1.rearrange("p h n -> p (h n)"), ALU.add))
                        nc.vector.tensor_scalar(hid[:, t, 0:GRP], hid[:, t, 0:GRP], LIMIT, None, ALU.min).then_inc(glu_made, 1)
                        own(nc.vector.tensor_scalar(hid[:, t, GRP:2 * GRP], hid[:, t, GRP:2 * GRP], LIMIT, -LIMIT, ALU.min, ALU.max))

                    def activated(t):
                        lin = hid[:, t, GRP:2 * GRP]
                        dve.wait_ge(glu_made, n * TG + (t + 1))
                        own(nc.vector.scalar_tensor_tensor(out=lin, in0=lin, scalar=1.0, in1=hid[:, t, 0:GRP], op0=ALU.add, op1=ALU.mult))
                        dve.wait_ge(sig_made, n * TG + (t + 1))
                        nc.vector.tensor_tensor(act_v[:, t], lin, sig[:, t], ALU.mult).then_inc(act_made, 1)

                    dve.wait_ge(b1_in, (n + 1) * (16 * CG))
                    clamped(0)
                    clamped(1)
                    activated(0)
                    clamped(2)
                    activated(1)
                    activated(2)
                    assert k[0] == STEPS
                    dve.wait_ge(b2_in, (n + 1) * (16 * CG))
                    dve.wait_ge(y_stored, n * (16 * TG))
                    for t in range(TG):
                        dve.wait_ge(y_mm, n * TG + (t + 1))
                        nc.vector.tensor_tensor(y_out[:, t], banks[:, 3 + t, 0:GRP], bias2, ALU.add).then_inc(y_made, 1)
            for i in range(TT):
                dve.wait_ge(y_loaded[i], 16)
                for j in range(TOPK):
                    ins = nc.vector.scalar_tensor_tensor(out=h_res[:, i], in0=y_in[:, i, j], scalar=gate_w[:, i, j:j + 1], in1=h_res[:, i],
                                                         op0=ALU.mult, op1=ALU.add)
                    if j < TOPK - 1:
                        chain(ins)
                    else:
                        ins.then_inc(summed, 1)
                if i:
                    scale_out(dve, i - 1)
            scale_out(dve, TT - 1)


_INS = ['x', 'meta_tokens', 'norm_mix_g', 'w_in', 'b_in', 'conv_dw_w', 'conv_dw_b', 'conv_ln_g', 'conv_ln_b',
        'conv_pw_w', 'conv_pw_b', 'mlstm_norm_g', 'mlstm_out_w', 'w_out', 'norm_ffn_g', 'router_w', 'router_b',
        'expert_w1', 'expert_b1', 'expert_w2', 'expert_b2', 'final_norm_g']
_OUTS = [((1, SEQ, D), 'float32')]


def kernel(**inputs):
    import numpy as _np
    import concourse.bacc as _bacc
    from concourse import mybir as _mybir
    from concourse.bass_utils import run_bass_kernel_spmd as _run

    nc = _bacc.Bacc("TRN2", target_bir_lowering=False, num_devices=1)
    arrays, args = {}, []
    for name in _INS:
        a = _np.ascontiguousarray(inputs[name])
        arrays[f"in_{name}_dram"] = a
        args.append(nc.dram_tensor(f"in_{name}_dram", a.shape, _mybir.dt.from_np(a.dtype), kind="ExternalInput").ap())
    for i, (shape, dtype) in enumerate(_OUTS):
        dt = _mybir.dt.from_np(_np.dtype(dtype))
        args.append(nc.dram_tensor(f"out_{i}_dram", shape, dt, kind="ExternalOutput").ap())
    hybrid_block(nc, *args)
    r = _run(nc, [arrays], core_ids=[0])
    return r.results[0]["out_0_dram"]
```

```python
import concourse.bass as bass
from concourse import mybir
from contextlib import ExitStack
import numpy as np

F32 = mybir.dt.float32
F32R = mybir.dt.float32r
BF16 = mybir.dt.bfloat16
I32 = mybir.dt.int32
U32 = mybir.dt.uint32
ACT = mybir.ActivationFunctionType
ALU = mybir.AluOpType
AX = mybir.AxisListType

P = 128
D = 1024
SEQ = 512
META = 16
NT = META + SEQ
HALF = NT // 2
KT = D // P
TT = SEQ // P
HEADS = 4
DV = D // HEADS
DK = DV // 2
VW = DV + 1
CHUNKS = TT + 1
CONV_W = 31
CONV_STEPS = CONV_W + 1
EARLY_TAPS = 4
PADL = CONV_W - 1 - META
CIN = PADL + NT
QK_SCALE = DK ** -0.5
EPS = 1e-5
NE = 32
TOPK = 4
DFF = D
ALPHA = 1.702
LIMIT = 7.0
GRP = 256
GT = GRP // P
MASKED = 1.0e30

GATE_OFF = D
Q_OFF = 2 * D
K_OFF = Q_OFF + HEADS * DK
V_OFF = K_OFF + HEADS * DK
I_OFF = V_OFF + D
F_OFF = I_OFF + HEADS
O_OFF = F_OFF + HEADS
GC_OFF = O_OFF + D
GM_OFF = GC_OFF + D
F_ROW = 32
W_ROW, FLOOR_ROW = 32, 64
ROWS = 96

GLU_PAIR, QK_PAIR, V_PAIR, SIG_PAIR, PW_PAIR, OW_PAIR, WO_PAIR = 0, 4, 6, 8, 14, 16, 18

B_A, B_Q, B_SIG, LN_G, LN_B, PW_B, MN_G, DW_B = 0, 16, 24, 48, 56, 64, 72, 80
VEC_ROWS = 88
N_VECS = 12

SLOTS = 96
TG = SLOTS // 32
CG = 4
PASSES = -(-SEQ // SLOTS)
PARTS = 3
NONE = 1 << 14
RING = 12
W1C = KT
LATE = 3
RC = DFF * 2


SILU_TILES = ((0, 1), (2, 3, 4), (5, 6, 7), ())
PW_BANKS = (2, 3, 6, 7)


def chunk_span(c):
    return (0, META) if c == 0 else (META + P * (c - 1), META + P * c)


def hybrid_block(nc, x, meta_tokens, norm_mix_g, w_in, b_in, conv_dw_w, conv_dw_b, conv_ln_g, conv_ln_b,
                 conv_pw_w, conv_pw_b, mlstm_norm_g, mlstm_out_w, w_out, norm_ffn_g, router_w, router_b,
                 expert_w1, expert_b1, expert_w2, expert_b2, final_norm_g, out):
    ctx = ExitStack()
    with ctx:
        def sem(name):
            return ctx.enter_context(nc.semaphore(name))

        base = -(-nc.sbuf_base // 32) * 32
        limit = nc.sbuf_usable_end
        top = [base]

        def at(name, shape, dt, offset):
            return nc.alloc_sbuf_tensor_at(name, shape, dt, offset=offset).ap()

        def size(shape, dt=F32):
            return -(-int(np.prod(shape[1:])) * mybir.dt.size(dt) // 32) * 32

        def take(name, shape, dt=F32):
            off = top[0]
            top[0] += size(shape, dt)
            return at(name, shape, dt, off), off

        chan = size([P, KT, SEQ])
        stage, stage_at = take("stage", [P, 2, KT, GRP])
        w_hi, _ = take("w_hi", [P, 2, KT, GRP], F32R)
        w_lo, _ = take("w_lo", [P, 2, KT, GRP], F32R)
        u_hi, u_hi_at = take("u_hi", [P, KT, NT], F32R)
        gates_at = top[0]
        gates = at("gates", [P, 3 * KT, SEQ], F32, gates_at)
        top[0] += 2 * chan
        conv_in, _ = take("conv_in", [P, KT, CIN])
        u_lo, u_lo_at = take("u_lo", [P, KT, NT], F32R)
        conv, conv_at = take("conv", [P, KT, SEQ])
        q_sb, q_at = take("q_sb", [P, HEADS, SEQ])
        k_sb, _ = take("k_sb", [P, HEADS, NT])
        v_sb, v_at = take("v_sb", [P, TT, HEADS, VW])
        v_meta, _ = take("v_meta", [META, HEADS, VW])
        ring_end = top[0]
        probs, probs_at = take("probs", [P, HEADS, SEQ])
        state, state_at = take("state", [P, HEADS, VW])
        kw_sb, kw_at = take("kw_sb", [P, HEADS, DK])
        h_tok, h_tok_at = take("h_tok", [P, HEADS, DV])
        cols, _ = take("cols", [P, CHUNKS, ROWS])
        decay, _ = take("decay", [P, HEADS, TT])
        ident, _ = take("ident", [P, P])
        mean_w, _ = take("mean_w", [P, P])
        maskpos, _ = take("maskpos", [P, P])
        taps, _ = take("taps", [P, KT, CONV_W])
        vec, _ = take("vec", [P, VEC_ROWS])
        small, _ = take("small", [P, 64])
        assert top[0] <= limit, (top[0], limit)

        x_sb = at("x_sb", [P, TT, D], F32, gates_at)
        g_bc = at("g_bc", [P, D], F32, gates_at + chan)
        meta_sb = at("meta_sb", [META, D], F32, gates_at + chan + size([P, D]))
        square_out = at("square_out", [P, D], F32, gates_at + chan + 2 * size([P, D]))
        vec_rows = at("vec_rows", [VEC_ROWS, P], F32, conv_at)
        tap_rows = at("tap_rows", [CONV_W, D], F32, conv_at + size([P, P]))
        wif = at("wif", [P, KT, P], F32, v_at)
        wif_hi = at("wif_hi", [P, KT, P], F32R, v_at + size([P, KT, P]))
        wif_lo = at("wif_lo", [P, KT, P], F32R, v_at + 2 * size([P, KT, P]))
        rows_at, row = v_at + 3 * size([P, KT, P]), size([HEADS, NT])
        i_row = at("i_row", [HEADS, NT], F32, rows_at)
        f_row = at("f_row", [HEADS, NT], F32, rows_at + row)
        t_row = at("t_row", [HEADS, NT], F32, rows_at + 2 * row)
        keep_row = at("keep_row", [HEADS, NT], F32, q_at)
        b_row = at("b_row", [HEADS, NT], F32, q_at + row)
        e_row = at("e_row", [HEADS, NT], F32, q_at + 2 * row)
        sg = at("sg", [P, 2, HALF], F32, probs_at)
        vb_bc = at("vb_bc", [P, D], F32, probs_at + size([P, D]))
        gate_rows = at("gate_rows", [P, NT], F32, state_at)
        m_row = at("m_row", [HEADS, NT], F32, state_at + row)
        inter_row = at("inter_row", [HEADS, NT], F32, state_at + 2 * row)
        squares = at("squares", [P, KT, SEQ], F32, gates_at + 2 * chan)
        channel_sum = at("channel_sum", [P, SEQ], F32, h_tok_at + size([P, SEQ]))
        odd_taps = at("odd_taps", [P, SEQ], F32, h_tok_at + size([P, SEQ]))
        square_total = at("square_total", [P, SEQ], F32, h_tok_at + size([P, SEQ]))
        silu_hi = at("silu_hi", [P, KT, SEQ], F32R, u_hi_at)
        silu_lo = at("silu_lo", [P, KT, SEQ], F32R, conv_at)
        h_hi = at("h_hi", [P, KT, SEQ], F32R, u_lo_at)
        h_lo = at("h_lo", [P, KT, SEQ], F32R, gates_at + chan)
        mix_hi = at("mix_hi", [P, KT, SEQ], F32R, u_hi_at)
        mix_lo = at("mix_lo", [P, KT, SEQ], F32R, gates_at)
        h_res = at("h_res", [P, TT, D], F32, probs_at)
        GC, OG, GM = 0, KT, 2 * KT

        chunk = size([P, RC])
        w1_ring = [at(f"w1_ring{c}", [P, 2, DFF], F32, ring_end - chunk * (c + 1)) for c in range(W1C)]
        w2_ring = [at(f"w2_ring{c}", [P, 2, D], F32, ring_end - chunk * (W1C + c + 1)) for c in range(RING - W1C)]
        assert ring_end - chunk * RING >= gates_at + chan
        low = [gates_at + chan]

        def under_ring(name, shape, dt=F32):
            off = low[0]
            low[0] += size(shape, dt)
            assert low[0] <= ring_end - chunk * RING
            return at(name, shape, dt, off)

        w_router = under_ring("w_router", [P, KT, NE])
        logits = under_ring("logits", [P, TT, NE])
        rb_bc = under_ring("rb_bc", [P, NE])
        best = under_ring("best", [P, TT, 8])
        best_idx = under_ring("best_idx", [P, TT, 8], U32)
        gate_w = under_ring("gate_w", [P, TT, TOPK])
        expert_f = under_ring("expert_f", [P, TT, TOPK])
        gate_sum = under_ring("gate_sum", [P, TT])
        n_passes = under_ring("n_passes", [P, 1], I32)
        count_max = under_ring("count_max", [P, 1])
        over = under_ring("over", [P, 8])
        carrier = under_ring("carrier", [1, 2 + TG])

        ffn_at = [stage_at]

        def in_stage(name, shape, dt=F32):
            off = ffn_at[0]
            ffn_at[0] += size(shape, dt)
            return at(name, shape, dt, off)

        u2 = in_stage("u2", [P, 2, D])
        gf_bc = in_stage("gf_bc", [P, D])
        assert ffn_at[0] <= stage_at + 2 * size([P, KT, GRP])
        one_hot = in_stage("one_hot", [P, TT, TOPK, NE])
        picked = in_stage("picked", [P, TT, TOPK, NE])
        mask = in_stage("mask", [P, TT, NE], BF16)
        place = in_stage("place", [P, TT, TOPK])
        dest = in_stage("dest", [P, TT * TOPK], I32)
        code = in_stage("code", [P, TT * TOPK], I32)
        expert_id = in_stage("expert_id", [P, NE])
        earlier = in_stage("earlier", [P, P], BF16)
        all_ones = in_stage("all_ones", [P, P], BF16)
        steps96 = in_stage("steps96", [P, PASSES - 1])
        no_code = in_stage("no_code", [SLOTS, PASSES * NE], I32)
        group_of = in_stage("group_of", [P, 1])
        token_of = in_stage("token_of", [SLOTS, PASSES * NE + 2], I32)
        row_of = in_stage("row_of", [P, TG, PASSES * NE + 1], I32)
        token_now = in_stage("token_now", [SLOTS, 1], I32)
        row_now = in_stage("row_now", [P, TG], I32)
        xs = in_stage("xs", [SLOTS, D])
        xT = in_stage("xT", [P, KT, SLOTS])
        hid = in_stage("hid", [P, TG, 2 * GRP])
        sig = in_stage("sig", [P, TG, GRP])
        act_v = in_stage("act_v", [P, TG, GRP])
        actT = in_stage("actT", [P, KT, SLOTS])
        y_out = in_stage("y_out", [P, TG, GRP])
        bias1 = in_stage("bias1", [P, 2, GRP])
        bias2 = in_stage("bias2", [P, GRP])
        last_g = in_stage("last_g", [P, D])
        u2T = in_stage("u2T", [P, 2, KT, P])
        bias_rest = in_stage("bias_rest", [PARTS * NE, 3 * D])
        bias_parts = in_stage("bias_parts", [PARTS * NE, 3 * D], BF16)
        expert_row = in_stage("expert_row", [PARTS * NE, NE + 1], BF16)
        row_pick = in_stage("row_pick", [PARTS * NE, 32], BF16)
        assert ffn_at[0] <= gates_at + chan
        y_in = at("y_in", [P, TT, TOPK, D], F32, ring_end - TT * TOPK * size([P, D]))

        u2_dram = nc.dram_tensor("u2_rows", [SEQ, D], F32).ap()
        y_dram = nc.dram_tensor("y_rows", [SEQ * TOPK * CG, GRP], F32).ap()
        table = nc.dram_tensor("slot_table", [PASSES * SLOTS * NE, 1], I32).ap()

        square_sum = small[:, 0:5]
        row_rstd = small[:, 5:10]
        minus_half = small[:, 10:11]
        if_bias = small[:, 11:12]
        m_prev = small[0:HEADS, 12:17]
        minus_m_end = small[0:HEADS, 17:22]
        den_inv = small[:, 22:26]
        head_square = small[:, 26:30]
        head_rstd = small[:, 30:34]
        head_scale = small[:, 34:38]
        q_bias = small[:, 38:42]
        h_square = small[:, 42:46]
        h_rstd = small[:, 46:50]
        f_square = small[:, 50:54]
        f_rstd = small[:, 54:58]
        ln_rstd = small[:, 58:62]

        banks = ctx.enter_context(nc.psum_tensor("banks", [P, 8, 512], F32)).ap()

        x_in = [sem(f"x_in{i}") for i in range(TT)]
        meta_in, g_in, vecs_in, ifw_in, vb_in = sem("meta_in"), sem("g_in"), sem("vecs_in"), sem("ifw_in"), sem("vb_in")
        consts_made, ifw_zeroed = sem("consts_made"), sem("ifw_zeroed")
        squared, rstd_made, scaled = sem("squared"), sem("rstd_made"), sem("scaled")
        u_transposed, u_hi_made, u_lo_made = sem("u_transposed"), sem("u_hi_made"), sem("u_lo_made")
        vecs_transposed, vecs_made = sem("vecs_transposed"), sem("vecs_made")
        ifw_hi_made, ifw_lo_made, if_mm, if_rows = sem("ifw_hi_made"), sem("ifw_lo_made"), sem("if_mm"), sem("if_rows")
        w_in_sem = [sem("w_loaded0"), sem("w_loaded1")]
        w_hi_made = [sem("w_hi_made0"), sem("w_hi_made1")]
        w_lo_made = [sem("w_lo_made0"), sem("w_lo_made1")]
        mm_done = sem("mm_done")
        glu_sig = sem("glu_sig")
        glu_out = [sem("glu_out0"), sem("glu_out1")]
        qk_out, v_out = sem("qk_out"), sem("v_out")
        sig_out = [sem(f"sig_out{t}") for t in range(4)]
        conv_step, dve_step, act_step, pool_step = sem("conv_step"), sem("dve_step"), sem("act_step"), sem("pool_step")
        abs_f, softplus, m_rows, gate_rows_made = sem("abs_f"), sem("softplus"), sem("m_rows"), sem("gate_rows_made")
        ln_mm, centered, squares_made, summed_up, var_made, rstd_bc_made = sem("ln_mm"), sem("centered"), sem("squares_made"), sem("summed_up"), sem("var_made"), sem("rstd_bc_made")
        normed, silu_made, silu_hi_made, silu_lo_made = sem("normed"), sem("silu_made"), sem("silu_hi_made"), sem("silu_lo_made")
        cols_mm, cols_made = sem("cols_mm"), sem("cols_made")
        head_mm, e_made, d_made, head_out = sem("head_mm"), sem("e_made"), sem("d_made"), sem("head_out")
        kt_mm, kw_made, outer_mm, state_out = sem("kt_mm"), sem("kw_made"), sem("outer_mm"), sem("state_out")
        h_mm, den_made, h_squared, h_scaled, tok_made = sem("h_mm"), sem("den_made"), sem("h_squared"), sem("h_scaled"), sem("tok_made")
        ht_mm, ht_gated, h_hi_made, h_lo_made, og_made = sem("ht_mm"), sem("ht_gated"), sem("h_hi_made"), sem("h_lo_made"), sem("og_made")
        pw_out, ow_out, mixed, mix_hi_made, mix_lo_made = sem("pw_out"), sem("ow_out"), sem("mixed"), sem("mix_hi_made"), sem("mix_lo_made")
        res_in, wo_out = sem("res_in"), sem("wo_out")
        stored = sem("stored")
        gf_in, router_in, u2_made, u2_stored = sem("gf_in"), sem("router_in"), sem("u2_made"), [sem(f"u2_stored{i}") for i in range(TT)]
        u2_mm, u2T_made, logits_mm, place_mm = sem("u2_mm"), sem("u2T_made"), sem("logits_mm"), sem("place_mm")
        moe_consts, mask_made, dest_made, table_set, table_written = sem("moe_consts"), sem("mask_made"), sem("dest_made"), sem("table_set"), sem("table_written")
        table_in, tables_made, passes_made, shifted, gate_exp = sem("table_in"), sem("tables_made"), sem("passes_made"), sem("shifted"), sem("gate_exp")
        ring_in = [sem(f"ring_in{c}") for c in range(RING)]
        ring_used = [sem(f"ring_used{c}") for c in range(RING)]
        xs_in, xs_used, xT_made, idx_step = sem("xs_in"), sem("xs_used"), sem("xT_made"), sem("idx_step")
        hid_mm, glu_made, sig_made, act_made, act_mm, actT_made = sem("hid_mm"), sem("glu_made"), sem("sig_made"), sem("act_made"), sem("act_mm"), sem("actT_made")
        y_mm, y_made, y_stored, ffn_step = sem("y_mm"), sem("y_made"), sem("y_stored"), sem("ffn_step")
        bias_split, rows_in = sem("bias_split"), sem("rows_in")
        bias_in, bias_mm, bias_made = sem("bias_in"), sem("bias_mm"), sem("bias_made")
        y_loaded = [sem(f"y_loaded{i}") for i in range(TT + 1)]
        last_g_in, summed, out_made = sem("last_g_in"), sem("summed"), sem("out_made")

        PAIR_TICKS = 8

        def pair_tick(n, k):
            return n * PAIR_TICKS + (PAIR_TICKS + k)

        def w_source(stage_pair, s, j):
            m, a0, b0, step = {
                GLU_PAIR: (w_in[0], 0, GATE_OFF, GRP),
                QK_PAIR: (w_in[0], Q_OFF, K_OFF, GRP),
                V_PAIR: (w_in[0], V_OFF, V_OFF + GRP, 2 * GRP),
                PW_PAIR: (conv_pw_w[0], 0, GRP, 2 * GRP),
                OW_PAIR: (mlstm_out_w[0], 0, GRP, 2 * GRP),
                WO_PAIR: (w_out[0], 0, GRP, 2 * GRP),
            }[stage_pair]
            return m.rearrange("(k p) n -> p k n", p=P)[:, :, bass.ds(j * step + (b0 if s else a0), GRP)]

        SIG_OFFS = (GC_OFF, O_OFF, GM_OFF)

        IDX = 3 + TG

        last_part = slice(NE * (PARTS - 1), NE * PARTS)
        block = ctx.enter_context(nc.Block())

        @block.sync
        def _(sp):
            def load_pair(n, source, first=False):
                for s in range(2):
                    if not first:
                        sp.wait_ge(w_lo_made[s], n)
                    sp.dma_start(stage[:, s], source(s)).then_inc(w_in_sem[s], 16)

            xt = x[0].rearrange("(i p) d -> i p d", p=P)
            for i in range(TT):
                sp.dma_start(x_sb[:, i], xt[i]).then_inc(x_in[i], 16)
            sp.dma_start(meta_sb, meta_tokens).then_inc(meta_in, 16)
            load_pair(0, lambda s: w_source(GLU_PAIR, s, 0), first=True)
            b2 = b_in[0]
            rows = [(B_A, b2[0:V_OFF], V_OFF // P), (B_SIG, b2[GC_OFF:GC_OFF + D], KT), (B_SIG + KT, b2[O_OFF:O_OFF + D], KT),
                    (B_SIG + 2 * KT, b2[GM_OFF:GM_OFF + D], KT), (LN_G, conv_ln_g[0], KT), (LN_B, conv_ln_b[0], KT),
                    (PW_B, conv_pw_b[0], KT), (MN_G, mlstm_norm_g[0], KT), (DW_B, conv_dw_b[0], KT)]
            for r, src, n in rows:
                sp.dma_start(vec_rows[r:r + n], src.rearrange("(r c) -> r c", c=P)).then_inc(vecs_in, 16)
            sp.dma_start(tap_rows, conv_dw_w[0]).then_inc(vecs_in, 16)
            with nc.allow_non_contiguous_dma(reason="8 biases"):
                for r, off in ((0, I_OFF), (F_ROW, F_OFF)):
                    sp.dma_start(if_bias[r:r + HEADS], b2[off:off + HEADS].rearrange("(r c) -> r c", c=1)).then_inc(vecs_in, 16)
            sp.dma_start(vb_bc, b_in[:, V_OFF:V_OFF + D].to_broadcast([P, D])).then_inc(vb_in, 16)
            with sp.Fori(1, 4) as j:
                load_pair(j, lambda s: w_source(GLU_PAIR, s, j))
            for stage_pair in (QK_PAIR, V_PAIR):
                for j in range(2):
                    load_pair(stage_pair + j, lambda s: w_source(stage_pair, s, j))
            win = w_in[0].rearrange("(k p) n -> p k n", p=P)
            for g, off in enumerate(SIG_OFFS):
                for j in range(2):
                    load_pair(SIG_PAIR + 2 * g + j, lambda s: win[:, :, off + (2 * j + s) * GRP:off + (2 * j + s + 1) * GRP])
            for stage_pair in (PW_PAIR, OW_PAIR):
                for j in range(2):
                    load_pair(stage_pair + j, lambda s: w_source(stage_pair, s, j))

            def load_chunk(e, c):
                if c < W1C:
                    src = expert_w1[0, bass.ds(e, 1), P * c:P * (c + 1), :].rearrange("e p (g n) -> p (e g) n", g=2)
                    sp.dma_start(w1_ring[c], src).then_inc(ring_in[c], 16)
                else:
                    m = c - W1C
                    src = expert_w2[0, bass.ds(e, 1), 2 * P * m:2 * P * (m + 1), :].rearrange("e (k p) n -> p (e k) n", p=P)
                    sp.dma_start(w2_ring[m], src).then_inc(ring_in[c], 16)

            sp.wait_ge(h_lo_made, 2 * TT)
            sp.dma_start(h_res, x[0].rearrange("(i p) d -> p i d", p=P)).then_inc(res_in, 16)
            for c in range(4):
                load_chunk(0, c)
            load_pair(WO_PAIR, lambda s: w_source(WO_PAIR, s, 0))
            sp.wait_ge(mm_done, pair_tick(PW_PAIR + 1, 8))
            for c in range(4, 6):
                load_chunk(0, c)
            load_pair(WO_PAIR + 1, lambda s: w_source(WO_PAIR, s, 1))
            sp.wait_ge(mm_done, pair_tick(OW_PAIR + 1, 8))
            sp.wait_ge(mixed, KT)
            for c in range(6, RING):
                load_chunk(0, c)
            sp.dma_start(w_router, router_w[0].rearrange("(k p) e -> p k e", p=P)).then_inc(router_in, 16)
            sp.dma_start(rb_bc, router_b.to_broadcast([P, NE])).then_inc(router_in, 16)
            for s in range(2):
                sp.wait_ge(w_lo_made[s], WO_PAIR + 2)
            sp.dma_start(gf_bc, norm_ffn_g.to_broadcast([P, D])).then_inc(gf_in, 16)
            for i in range(TT):
                sp.wait_ge(u2_made, i + 1)
                sp.dma_start(u2_dram[P * i:P * (i + 1)], u2[:, i % 2]).then_inc(u2_stored[i], 16)
            sp.wait_ge(moe_consts, 1)
            sp.dma_start(table.rearrange("(q i e) o -> i q (e o)", i=SLOTS, e=NE),
                         no_code.rearrange("i (q e) -> i q e", e=NE)).then_inc(table_set, 16)
            sp.wait_ge(mm_done, pair_tick(WO_PAIR + 1, 8))
            for m in range(PARTS):
                sp.dma_start(bias_rest[NE * m:NE * (m + 1), 0:2 * D], expert_b1[0]).then_inc(bias_in, 16)
                sp.dma_start(bias_rest[NE * m:NE * (m + 1), 2 * D:3 * D], expert_b2[0]).then_inc(bias_in, 16)
            sp.wait_ge(table_written, 16 * TT * TOPK)
            by_slot = table.rearrange("(q i e) o -> i q (e o)", i=SLOTS, e=NE)
            sp.dma_start(token_of[:, 0:PASSES * NE].rearrange("i (q e) -> i q e", e=NE), by_slot).then_inc(table_in, 16)
            for g in range(CG):
                for t in range(TG):
                    sp.dma_start(row_of[32 * g:32 * (g + 1), t, 0:PASSES * NE].rearrange("i (q e) -> i q e", e=NE),
                                 by_slot[32 * t:32 * (t + 1)]).then_inc(rows_in, 16)
            sp.dma_start(last_g, final_norm_g.rearrange("(a d) -> a d", a=1).to_broadcast([P, D])).then_inc(last_g_in, 16)

            def load_block(n, e):
                for c in range(RING):
                    if c in (W1C - 1, RING - 1):
                        sp.wait_ge(hid_mm if c < W1C else y_mm, n * TG)
                    else:
                        sp.wait_ge(ring_used[c], n)
                    load_chunk(e, c)

            with sp.Fori(1, NE) as e:
                load_block(e, e)
            sp.wait_ge(passes_made, 1)
            passes = sp.value_load(n_passes[0:1, 0:1], min_val=1, max_val=PASSES)
            with sp.If(passes > 1):
                with sp.Fori(1, passes) as q:
                    with sp.Fori(0, NE) as e:
                        load_block(q * NE + e, e)
            sp.wait_ge(y_stored, passes * (16 * TG * NE))
            results = y_dram.rearrange("(i p r) n -> i p (r n)", i=TT, p=P)
            for n, (i, a, b) in enumerate([(i, 0, TOPK) for i in range(TT - 1)] + [(TT - 1, 0, 2), (TT - 1, 2, TOPK)]):
                sp.dma_start(y_in[:, i, a:b], results[i].rearrange("p (k d) -> p k d", k=TOPK)[:, a:b]).then_inc(y_loaded[n], 16)
            for i in range(TT):
                sp.wait_ge(out_made, i + 1)
                sp.dma_start(out[0, P * i:P * (i + 1), :], h_res[:, i]).then_inc(stored, 16)
            sp.wait_ge(stored, 16 * TT)

        @block.gpsimd
        def _(pool):
            steps = [0]

            def chain(ins):
                steps[0] += 1
                ins.then_inc(pool_step, 1)
                pool.wait_ge(pool_step, steps[0])

            for t in range(4):
                pool.sem_inc(sig_out[t], 1)
            pool.sem_inc(head_out, 1)
            pool.sem_inc(y_made, 1)
            for c in range(GT):
                pool.sem_inc(glu_out[c], 1)
            nc.gpsimd.memset(minus_half, -0.5).then_inc(mm_done, PAIR_TICKS)
            nc.gpsimd.memset(wif, 0.0).then_inc(ifw_zeroed, 1)
            nc.gpsimd.memset(ident, 0.0)
            chain(nc.gpsimd.memset(maskpos, 0.0))
            nc.gpsimd.affine_select(out=ident, in_=ident, compare_op=ALU.not_equal, fill=1.0, base=0,
                                    pattern=[[-1, P]], channel_multiplier=1).then_inc(consts_made, 1)
            nc.gpsimd.affine_select(out=maskpos, in_=maskpos, compare_op=ALU.is_ge, fill=MASKED, base=0,
                                    pattern=[[1, P]], channel_multiplier=-1).then_inc(consts_made, 1)
            nc.gpsimd.memset(mean_w, 1.0 / D).then_inc(consts_made, 1)
            nc.gpsimd.memset(conv_in[:, :, 0:PADL], 0.0).then_inc(consts_made, 1)
            nc.gpsimd.memset(gate_rows, 0.0).then_inc(consts_made, 1)
            nc.gpsimd.memset(keep_row, 1.0).then_inc(consts_made, 1)
            pool.wait_ge(ifw_zeroed, 1)
            with nc.allow_non_contiguous_dma(reason="4 columns of each row"):
                for off, col in ((I_OFF, 0), (F_OFF, F_ROW)):
                    pool.dma_start(wif[:, :, col:col + HEADS],
                                   w_in[0].rearrange("(k p) n -> p k n", p=P)[:, :, off:off + HEADS]).then_inc(ifw_in, 16)

            def rstd(rows, sums, to, n, done=None):
                chain(nc.gpsimd.tensor_scalar(to, sums, 1.0 / n, EPS, ALU.mult, ALU.add))
                ins = nc.gpsimd.tensor_tensor(to, to, minus_half[0:rows].to_broadcast([rows, to.shape[1]]), ALU.pow)
                if done is None:
                    chain(ins)
                else:
                    ins.then_inc(done, 1)

            for i in range(CHUNKS):
                rows = P if i < TT else META
                pool.wait_ge(squared, i + 1)
                rstd(rows, square_sum[0:rows, i:i + 1], row_rstd[0:rows, i:i + 1], D, rstd_made)
            pool.wait_ge(ifw_hi_made, 1)
            nc.gpsimd.tensor_tensor(wif_lo, wif, wif_hi.bitcast(F32), ALU.subtract).then_inc(ifw_lo_made, 1)

            def split_pair(n):
                for s in range(2):
                    pool.wait_ge(w_hi_made[s], n + 1)
                    pool.wait_ge(mm_done, pair_tick(n, 8 if s else 2) - PAIR_TICKS)
                    nc.gpsimd.tensor_tensor(w_lo[:, s], stage[:, s], w_hi[:, s].bitcast(F32),
                                            ALU.subtract).then_inc(w_lo_made[s], 1)

            with pool.Fori(0, PW_PAIR - 1) as n:
                split_pair(n)
            pool.wait_ge(var_made, 1)
            nc.gpsimd.tensor_tensor(ln_rstd, ln_rstd, minus_half.to_broadcast([P, TT]), ALU.pow).then_inc(rstd_bc_made, 1)
            split_pair(PW_PAIR - 1)
            for t in range(KT):
                pool.wait_ge(sig_out[t % 4], OG // 4 + t // 4 + 2)
                og = gates[:, OG + t]
                nc.gpsimd.tensor_scalar(og, og, vec[:, MN_G + t:MN_G + t + 1], None, ALU.mult).then_inc(og_made, 1)
            split_pair(PW_PAIR)
            for i in range(TT):
                pool.wait_ge(h_squared, HEADS * (i + 1))
                rstd(P, head_square, head_rstd, DV)
                nc.gpsimd.tensor_tensor(head_scale, head_rstd, den_inv, ALU.mult).then_inc(h_scaled, 1)
            with pool.Fori(PW_PAIR + 1, WO_PAIR + 2) as n:
                split_pair(n)

            def ffn_norm(i):
                pool.wait_ge(squared, CHUNKS + i + 1)
                rstd(P, h_square[:, i:i + 1], h_rstd[:, i:i + 1], D, rstd_made)

            ffn_norm(0)
            ffn_norm(1)
            pool.wait_ge(mm_done, pair_tick(WO_PAIR + 1, 8))
            nc.gpsimd.memset(no_code, NONE).then_inc(moe_consts, 1)
            nc.gpsimd.iota(code, [[TOPK * P, TT], [1, TOPK]], base=0, channel_multiplier=TOPK)
            nc.gpsimd.iota(expert_id, [[1, NE]], base=0, channel_multiplier=0, allow_small_or_imprecise_dtypes=True)
            chain(nc.gpsimd.iota(steps96, [[SLOTS, PASSES - 1]], base=SLOTS, channel_multiplier=0, allow_small_or_imprecise_dtypes=True))
            for g in range(CG):
                chain(nc.gpsimd.memset(group_of[32 * g:32 * (g + 1)], float(g)))
            nc.gpsimd.memset(all_ones, 1.0)
            nc.gpsimd.memset(carrier, 0.0)
            nc.gpsimd.memset(token_of, NONE)
            nc.gpsimd.memset(row_of, NONE)
            nc.gpsimd.memset(xs, 0.0)
            chain(nc.gpsimd.memset(earlier, 1.0))
            nc.gpsimd.affine_select(out=earlier, in_=earlier, compare_op=ALU.is_gt, fill=0.0, base=0,
                                    pattern=[[1, P]], channel_multiplier=-1).then_inc(moe_consts, 1)
            ffn_norm(2)
            ffn_norm(3)
            for m in range(PARTS):
                chain(nc.gpsimd.tensor_copy(expert_row[NE * m:NE * (m + 1), 0:NE], ident[NE * m:NE * (m + 1), NE * m:NE * (m + 1)]))
            nc.gpsimd.tensor_copy(expert_row[:, NE:NE + 1], expert_row[:, 0:1]).then_inc(moe_consts, 1)
            pool.wait_ge(moe_consts, 3)
            pool.wait_ge(table_set, 16)
            for m in range(TT * TOPK):
                pool.wait_ge(dest_made, m // TOPK + 1)
                pool.indirect_dma_start(out=table, out_offset=bass.IndirectOffsetOnAxis(ap=dest[:, m:m + 1], axis=0),
                                        in_=code[:, m:m + 1], in_offset=None).then_inc(table_written, 16)

            pool.wait_ge(tables_made, 1)
            for i in range(TT):
                pool.wait_ge(u2_stored[i], 16)

            def gather(n, copied):
                nc.gpsimd.tensor_copy(token_now, token_of[:, bass.ds(n, 1)]).then_inc(idx_step, 1)
                pool.wait_ge(idx_step, copied)
                carry_wait(0)
                pool.indirect_dma_start(out=xs, out_offset=None, in_=u2_dram,
                                        in_offset=bass.IndirectOffsetOnAxis(ap=token_now, axis=0),
                                        bounds_check=last_token, oob_is_err=False).then_inc(xs_in, 16)

            def carry_wait(i):
                nc.gpsimd.tensor_tensor(carrier[:, 1 + i:2 + i], carrier[:, 0:1], carrier[:, 0:1], ALU.add).then_inc(idx_step, 1)

            last_token = pool.to_reg(SEQ - 1)
            last_row = pool.to_reg(SEQ * TOPK * CG - 1)
            gather(0, 1)
            pool.wait_ge(xs_used, 1)
            gather(1, 3)
            pool.wait_ge(tables_made, 2)
            passes = pool.value_load(n_passes[0:1, 0:1], min_val=1, max_val=PASSES)
            with pool.Fori(0, passes) as q:
                with pool.Fori(0, NE) as e:
                    n = q * NE + e
                    nc.gpsimd.tensor_copy(row_now, row_of[:, :, bass.ds(n, 1)].rearrange("p t o -> p (t o)")).then_inc(idx_step, 1)
                    pool.wait_ge(xs_used, n + 2)
                    gather(n + 2, n * IDX + 6)
                    for t in range(TG):
                        pool.wait_ge(y_made, n * TG + (t + 2))
                        carry_wait(1 + t)
                        pool.indirect_dma_start(out=y_dram, out_offset=bass.IndirectOffsetOnAxis(ap=row_now[:, t:t + 1], axis=0),
                                                in_=y_out[:, t], in_offset=None, bounds_check=last_row,
                                                oob_is_err=False).then_inc(y_stored, 16)
                    pool.wait_ge(y_stored, (n + 1) * (16 * TG))
            for i in range(TT):
                pool.wait_ge(squared, CHUNKS + TT + i + 1)
                rstd(P, f_square[:, i:i + 1], f_rstd[:, i:i + 1], D, rstd_made)

        def u2T_part(act, i):
            for f in range(2):
                act.wait_ge(u2_mm, 2 * i + f + 1)
                if i >= 2:
                    act.wait_ge(logits_mm, i - 1)
                nc.scalar.activation(u2T[:, i % 2, 4 * f:4 * f + 4], banks[:, 4 * (1 - i % 2) + f].rearrange("p (k t) -> p k t", t=P),
                                     ACT.Copy).then_inc(u2T_made, 1)

        @block.scalar
        def _(act):
            steps = [0]

            def chain(ins):
                steps[0] += 1
                ins.then_inc(act_step, 1)
                act.wait_ge(act_step, steps[0])

            act.dma_start(g_bc, norm_mix_g.to_broadcast([P, D])).then_inc(g_in, 16)

            def split_hi(n, s):
                act.wait_ge(w_in_sem[s], 16 * (n + 1))
                act.wait_ge(mm_done, pair_tick(n, 8 if s else 2) - PAIR_TICKS)
                nc.scalar.activation(w_hi[:, s], stage[:, s], ACT.Copy).then_inc(w_hi_made[s], 1)

            for i in range(CHUNKS):
                n = P if i < TT else META
                act.wait_ge(x_in[i] if i < TT else meta_in, 16)
                src = x_sb[:, i] if i < TT else meta_sb
                if i:
                    act.wait_ge(squared, i)
                nc.scalar.activation(square_out[0:n], src, ACT.Square, accum_out=square_sum[0:n, i:i + 1]).then_inc(squared, 1)
            for j in range(2 * TT + 1):
                act.wait_ge(u_transposed, j + 1)
                i, h = j // 2, j % 2
                dst, src = (u_hi[:, 4 * h:4 * h + 4, META + P * i:META + P * (i + 1)], banks[:, j % 4].rearrange("p (k t) -> p k t", t=P)) \
                    if i < TT else (u_hi[:, :, 0:META], banks[:, j % 4, 0:KT * META].rearrange("p (k t) -> p k t", t=META))
                nc.scalar.activation(dst, src, ACT.Copy).then_inc(u_hi_made, 1)
            act.wait_ge(ifw_in, 32)
            nc.scalar.activation(wif_hi, wif, ACT.Copy).then_inc(ifw_hi_made, 1)
            split_hi(0, 0)
            split_hi(0, 1)
            act.wait_ge(vecs_transposed, 1)
            nc.scalar.activation(vec, banks[:, 4, 0:VEC_ROWS], ACT.Copy).then_inc(vecs_made, 1)
            act.wait_ge(vecs_transposed, 2)
            nc.scalar.activation(taps, banks[:, 5, 0:KT * CONV_W].rearrange("p (k w) -> p k w", w=CONV_W), ACT.Copy).then_inc(vecs_made, 1)
            act.wait_ge(vecs_made, 1)
            nc.scalar.activation(q_bias, vec[:, B_Q:B_Q + HEADS], ACT.Copy, scale=QK_SCALE).then_inc(vecs_made, 1)
            act.wait_ge(if_mm, 1)
            act.wait_ge(vecs_in, 16 * N_VECS)
            for h in range(2):
                span = slice(HALF * h, HALF * (h + 1))
                nc.scalar.activation(f_row[:, span], banks[F_ROW:F_ROW + HEADS, 6 + h, 0:HALF], ACT.Identity,
                                     bias=if_bias[F_ROW:F_ROW + HEADS]).then_inc(if_rows, 1)
                nc.scalar.activation(i_row[:, span], banks[0:HEADS, 6 + h, 0:HALF], ACT.Identity,
                                     bias=if_bias[0:HEADS]).then_inc(if_rows, 1)
            act.wait_ge(abs_f, 1)
            chain(nc.scalar.activation(e_row, t_row, ACT.Exp, scale=-1.0))
            nc.scalar.activation(t_row, e_row, ACT.Ln, bias=1.0).then_inc(softplus, 1)
            act.wait_ge(m_rows, 1)
            for c in range(CHUNKS):
                a, b = chunk_span(c)
                nc.scalar.activation(gate_rows[W_ROW:W_ROW + HEADS, a:b], gate_rows[0:HEADS, a:b], ACT.Exp,
                                     bias=minus_m_end[:, c:c + 1]).then_inc(gate_rows_made, 1)
                if c:
                    nc.scalar.activation(inter_row[:, a:b], m_row[:, a:b], ACT.Exp, scale=-1.0,
                                         bias=m_prev[:, c:c + 1]).then_inc(gate_rows_made, 1)
            nc.scalar.activation(gate_rows[FLOOR_ROW:FLOOR_ROW + HEADS], b_row, ACT.Exp, scale=-1.0).then_inc(gate_rows_made, 1)

            with act.Fori(0, 4) as j:
                split_hi(j + 1, 0)
                for c in range(GT):
                    act.wait_ge(mm_done, pair_tick(j, 5 + 3 * c))
                    act.wait_ge(glu_out[1 - c], 2 * j + (2 * c + 1))
                    for h in range(2):
                        nc.scalar.activation(sg[:, h], banks[:, 4 * c + 2 + h, 0:HALF], ACT.Sigmoid,
                                             bias=vec[:, bass.ds(2 * j + (KT + c), 1)]).then_inc(glu_sig, 1)
                split_hi(j + 1, 1)
            for j in range(2):
                n = QK_PAIR + j
                for c in range(GT):
                    act.wait_ge(mm_done, pair_tick(n, 1 + c))
                    hd = 2 * j + c
                    nc.scalar.activation(q_sb[:, hd], banks[:, c], ACT.Identity, bias=q_bias[:, hd:hd + 1],
                                         scale=QK_SCALE).then_inc(qk_out, 1)
                split_hi(n + 1, 0)
                for c in range(GT):
                    act.wait_ge(mm_done, pair_tick(n, 5 + 3 * c))
                    hd = 2 * j + c
                    for h in range(2):
                        nc.scalar.activation(k_sb[:, hd, HALF * h:HALF * (h + 1)], banks[:, 2 + 2 * c + h, 0:HALF], ACT.Identity,
                                             bias=vec[:, B_Q + HEADS + hd:B_Q + HEADS + hd + 1]).then_inc(qk_out, 1)
                split_hi(n + 1, 1)
            for j in range(2):
                split_hi(V_PAIR + j + 1, 0)
                split_hi(V_PAIR + j + 1, 1)

            def sigmoid_pair(j):
                n = SIG_PAIR + j
                for s in range(2):
                    for c in range(GT):
                        act.wait_ge(mm_done, pair_tick(n, (5 + 3 * c) if s else 1 + c))
                        t = 2 * s + c
                        nc.scalar.activation(gates[:, bass.ds(4 * j + t, 1), :], banks[:, 4 + t:5 + t], ACT.Sigmoid,
                                             bias=vec[:, bass.ds(4 * j + (B_SIG + t), 1)]).then_inc(sig_out[t], 1)
                    split_hi(n + 1, s)

            act.wait_ge(cols_mm, 1)
            nc.scalar.activation(cols, banks[:, 1, 0:CHUNKS * ROWS].rearrange("p (c r) -> p c r", r=ROWS), ACT.Copy).then_inc(cols_made, 1)

            def head_exp(h):
                act.wait_ge(e_made, TT * (h + 1))
                nc.scalar.activation(probs[:, bass.ds(h, 1)], probs[:, bass.ds(h, 1)], ACT.Exp, scale=-1.0).then_inc(d_made, 1)

            with act.Fori(0, 2) as j:
                sigmoid_pair(j)
                head_exp(j)
            act.wait_ge(centered, 1)
            act.wait_ge(conv_step, CONV_STEPS * KT)
            nc.scalar.activation(squares, conv, ACT.Square).then_inc(squares_made, 1)
            with act.Fori(2, 4) as j:
                sigmoid_pair(j)
                head_exp(j)
            act.wait_ge(summed_up, 2)
            sigmoid_pair(4)
            for k in range(KT):
                act.wait_ge(normed, k + 1)
                nc.scalar.activation(conv[:, k], conv[:, k], ACT.Silu, scale=vec[:, LN_G + k:LN_G + k + 1],
                                     bias=vec[:, LN_B + k:LN_B + k + 1]).then_inc(silu_made, 1)
            sigmoid_pair(5)

            def scaled_keys(c):
                n = P if c else META
                act.wait_ge(kt_mm, c + 1)
                act.wait_ge(outer_mm, HEADS * c)
                for h in range(HEADS):
                    nc.scalar.activation(kw_sb[0:n, h], banks[0:n, 1, P * h:P * (h + 1)], ACT.Copy,
                                         scale=cols[0:n, c, W_ROW + h:W_ROW + h + 1]).then_inc(kw_made, 1)

            scaled_keys(0)
            for i in range(TT):
                act.wait_ge(den_made, i + 1)
                act.wait_ge(ht_mm, 2 * i)
                for h in range(HEADS):
                    nc.scalar.activation(h_tok[:, h], banks[:, 4 + h, 0:DV], ACT.Square, scale=den_inv[:, h:h + 1],
                                         accum_out=head_square[:, h:h + 1]).then_inc(h_squared, 1)
                if i + 1 < TT:
                    scaled_keys(i + 1)
                act.wait_ge(h_scaled, i + 1)
                act.wait_ge(h_squared, HEADS * (i + 1))
                for h in range(HEADS):
                    nc.scalar.activation(h_tok[:, h], banks[:, 4 + h, 0:DV], ACT.Copy,
                                         scale=head_scale[:, h:h + 1]).then_inc(tok_made, 1)
                for f in range(2):
                    act.wait_ge(ht_gated, 2 * i + f + 1)
                    nc.scalar.activation(h_hi[:, 4 * f:4 * f + 4, P * i:P * (i + 1)],
                                         gates[:, OG + 4 * f:OG + 4 * f + 4, P * i:P * (i + 1)], ACT.Copy).then_inc(h_hi_made, 1)
                act.wait_ge(silu_made, KT)
                act.wait_ge(mm_done, pair_tick(SIG_PAIR + 5, 8))
                for k in SILU_TILES[i]:
                    nc.scalar.activation(silu_hi[:, k], conv[:, k], ACT.Copy).then_inc(silu_hi_made, 1)
            for n in range(PW_PAIR, OW_PAIR + 1):
                for s in range(2):
                    split_hi(n + 1, s)
            for n in range(KT):
                if n == 4:
                    split_hi(WO_PAIR, 0)
                act.wait_ge(mixed, n + 1)
                nc.scalar.activation(mix_hi[:, n], gates[:, GC + n], ACT.Copy).then_inc(mix_hi_made, 1)
            split_hi(WO_PAIR, 1)
            for s in range(2):
                split_hi(WO_PAIR + 1, s)

            for s in range(2):
                act.wait_ge(w_lo_made[s], WO_PAIR + 2)
            for i in range(TT):
                act.wait_ge(wo_out, TT + i + 1)
                if i >= 2:
                    act.wait_ge(u2_stored[i - 2], 16)
                    act.wait_ge(u2_mm, 2 * (i - 1))
                nc.scalar.activation(u2[:, i % 2], h_res[:, i], ACT.Square, accum_out=h_square[:, i:i + 1]).then_inc(squared, 1)
                if i:
                    u2T_part(act, i - 1)
            u2T_part(act, TT - 1)
            act.wait_ge(bias_in, 16 * 2 * PARTS)
            nc.scalar.activation(bias_parts, bias_rest, ACT.Copy).then_inc(bias_split, 1)
            act.wait_ge(shifted, 1)
            nc.scalar.activation(gate_w, gate_w, ACT.Exp).then_inc(gate_exp, 1)
            act.wait_ge(bias_split, 2)
            for m in range(1, PARTS):
                nc.scalar.activation(bias_parts[NE * m:NE * (m + 1)], bias_rest[NE * m:NE * (m + 1)], ACT.Copy).then_inc(bias_split, 1)
            act.wait_ge(bias_split, PARTS + 2)
            nc.scalar.activation(bias_parts[last_part], bias_rest[last_part], ACT.Copy).then_inc(bias_split, 1)

            act.wait_ge(mm_done, pair_tick(WO_PAIR + 1, 8))
            act.wait_ge(xs_used, 1)
            for m in range(2):
                nc.scalar.activation(xT[:, 4 * m:4 * m + 4], banks[:, m, 0:4 * SLOTS].rearrange("p (k s) -> p k s", s=SLOTS),
                                     ACT.Copy).then_inc(xT_made, 1)

            def pick_rows(e):
                nc.scalar.activation(row_pick, expert_row[:, bass.ds(e, 1)].to_broadcast([PARTS * NE, 32]), ACT.Copy).then_inc(bias_made, 1)

            act.wait_ge(moe_consts, 3)
            pick_rows(0)
            act.wait_ge(passes_made, 1)
            passes = act.value_load(n_passes[0:1, 0:1], min_val=1, max_val=PASSES)
            with act.Fori(0, passes) as q:
                with act.Fori(0, NE) as e:
                    n = q * NE + e
                    act.wait_ge(bias_mm, n * 2 + 1)
                    nc.scalar.activation(bias1, banks[:, 3].rearrange("p (h n) -> p h n", h=2), ACT.Copy).then_inc(bias_made, 1)
                    act.wait_ge(bias_mm, n * 2 + 2)
                    nc.scalar.activation(bias2, banks[:, 4, 0:GRP], ACT.Copy).then_inc(bias_made, 1)
                    pick_rows(e + 1)

                    def sigmoid(t):
                        act.wait_ge(glu_made, n * TG + (t + 1))
                        nc.scalar.activation(sig[:, t], hid[:, t, 0:GRP], ACT.Sigmoid, scale=ALPHA).then_inc(sig_made, 1)

                    def take_actT(t):
                        act.wait_ge(act_mm, n * TG + (t + 1))
                        nc.scalar.activation(actT.rearrange("p (j h) s -> p h j s", h=2)[:, :, :, 32 * t:32 * (t + 1)],
                                             banks[:, 6 + t % 2, 0:2 * P].rearrange("p (h j s) -> p h j s", h=2, j=CG),
                                             ACT.Copy).then_inc(actT_made, 1)

                    sigmoid(0)
                    sigmoid(1)
                    take_actT(0)
                    take_actT(1)
                    sigmoid(2)
                    act.wait_ge(xs_used, n + 2)
                    for m in range(2):
                        nc.scalar.activation(xT[:, 4 * m:4 * m + 4], banks[:, m, 0:4 * SLOTS].rearrange("p (k s) -> p k s", s=SLOTS),
                                             ACT.Copy).then_inc(xT_made, 1)
                    take_actT(2)
            for i in range(TT):
                act.wait_ge(summed, i + 1)
                nc.scalar.activation(y_in[:, i, 0], h_res[:, i], ACT.Square, accum_out=f_square[:, i:i + 1]).then_inc(squared, 1)

        @block.tensor
        def _(pe):
            def product(dst, stationary, moving, k):
                a, b = stationary
                c, d = moving
                for n, (l, r) in enumerate(((a, c), (b, c), (a, d))):
                    last = nc.tensor.matmul(dst, l, r, start=(k == 0 and n == 0), stop=(k == KT - 1 and n == 2))
                return last

            def weights(s, k, c):
                return w_hi[:, s, k, P * c:P * (c + 1)], w_lo[:, s, k, P * c:P * (c + 1)]

            def channel_tile(s, c, src, dst, span, ticks=None):
                hi, lo = src
                for k in range(KT):
                    last = product(dst, weights(s, k, c), (hi[:, k, span], lo[:, k, span]), k)
                if ticks:
                    last.then_inc(mm_done, ticks)

            u = (u_hi, u_lo)
            halves = [slice(HALF * h, HALF * (h + 1)) for h in range(2)]
            main = slice(META, NT)

            pe.wait_ge(consts_made, 1)
            for j in range(2 * TT + 1):
                i, h = j // 2, j % 2
                pe.wait_ge(scaled, i + 1)
                if j >= 4:
                    pe.wait_ge(u_lo_made, j - 3)
                if i < TT:
                    for k in range(4):
                        col = P * (4 * h + k)
                        last = nc.tensor.transpose(banks[:, j % 4, P * k:P * (k + 1)], x_sb[:, i, col:col + P], ident)
                else:
                    for k in range(KT):
                        last = nc.tensor.transpose(banks[:, j % 4, META * k:META * (k + 1)], meta_sb[:, P * k:P * (k + 1)],
                                                   ident[0:META, 0:META])
                last.then_inc(u_transposed, 1)
            pe.wait_ge(vecs_in, 16 * N_VECS)
            nc.tensor.transpose(banks[:, 4, 0:VEC_ROWS], vec_rows, ident[0:VEC_ROWS, 0:VEC_ROWS]).then_inc(vecs_transposed, 1)
            for k in range(KT):
                last = nc.tensor.transpose(banks[:, 5, CONV_W * k:CONV_W * (k + 1)], tap_rows[:, P * k:P * (k + 1)],
                                           ident[0:CONV_W, 0:CONV_W])
            last.then_inc(vecs_transposed, 1)
            pe.wait_ge(u_lo_made, 2 * TT + 1)
            pe.wait_ge(ifw_lo_made, 1)
            for h in range(2):
                for k in range(KT):
                    last = product(banks[:, 6 + h, 0:HALF], (wif_hi[:, k], wif_lo[:, k]),
                                   (u_hi[:, k, halves[h]], u_lo[:, k, halves[h]]), k)
            last.then_inc(if_mm, 1)

            def wait_weights(n, s):
                pe.wait_ge(w_lo_made[s], n + 1)

            pe.wait_ge(if_rows, 4)
            pe.wait_ge(vecs_made, 2)
            with pe.Fori(0, 4) as j:
                for s in range(2):
                    wait_weights(j, s)
                    for c in range(GT):
                        pe.wait_ge(glu_out[c], 2 * j + 1)
                        for h in range(2):
                            channel_tile(s, c, u, banks[:, 4 * c + 2 * s + h, 0:HALF], halves[h],
                                         (3 if s else 1) if h else None)
            for j in range(2):
                for s in range(2):
                    wait_weights(QK_PAIR + j, s)
                    for c in range(GT):
                        pe.wait_ge(glu_out[0], 9)
                        if s and c:
                            pe.wait_ge(glu_out[1], 9)
                        if s == 0:
                            if j:
                                pe.wait_ge(qk_out, 1 + c)
                            channel_tile(0, c, u, banks[:, c], main, 1)
                        else:
                            if j:
                                pe.wait_ge(qk_out, 4 + 2 * c)
                            for h in range(2):
                                channel_tile(1, c, u, banks[:, 2 + 2 * c + h, 0:HALF], halves[h], 3 if h else None)

            def token_tile(s, src, dst, span, ticks=None):
                hi, lo = src
                for k in range(KT):
                    last = product(dst, (hi[:, k, span], lo[:, k, span]), (w_hi[:, s, k], w_lo[:, s, k]), k)
                if ticks:
                    last.then_inc(mm_done, ticks)

            pe.wait_ge(qk_out, 12)
            for j in range(2):
                for s in range(2):
                    wait_weights(V_PAIR + j, s)
                    for i in range(TT + 1):
                        if j and s == 0:
                            pe.wait_ge(v_out, i + 1)
                        span = slice(META + P * i, META + P * (i + 1)) if i < TT else slice(0, P)
                        token_tile(s, u, banks[:, i, GRP * s:GRP * (s + 1)], span,
                                   (2 if i == TT else 1) if s else (2 if i == TT else None))
            pe.wait_ge(v_out, 2 * (TT + 1))

            pe.wait_ge(gate_rows_made, 2 * CHUNKS)
            for c in range(CHUNKS):
                a = chunk_span(c)[0]
                last = nc.tensor.transpose(banks[:, 1, ROWS * c:ROWS * (c + 1)], gate_rows[0:ROWS, a:a + P], ident[0:ROWS, 0:ROWS])
            last.then_inc(cols_mm, 1)
            pe.wait_ge(cols_made, 1)

            def sigmoid_tiles(j):
                for s in range(2):
                    wait_weights(j + SIG_PAIR, s)
                    for c in range(GT):
                        t = 2 * s + c
                        pe.wait_ge(sig_out[t], j + 1)
                        channel_tile(s, c, u, banks[:, 4 + t], main, 3 if s else 1)

            def head(h):
                pe.wait_ge(head_out, h + 1)
                sel = ident[0:HEADS, h:h + 1].to_broadcast([HEADS, P])
                nc.tensor.matmul(banks[:, 1], sel, m_row[:, main], start=True, stop=True)
                nc.tensor.matmul(banks[:, 2], sel, inter_row[:, main], start=True, stop=True)
                for i in range(TT):
                    last = nc.tensor.matmul(banks[:, 3, P * i:P * (i + 1)], k_sb[:, h, META + P * i:META + P * (i + 1)],
                                            q_sb[:, h, P * i:P * (i + 1)], start=True, stop=True)
                last.then_inc(head_mm, 1)

            for j in range(2):
                sigmoid_tiles(j)
                head(j)
            pe.wait_ge(summed_up, 1)
            nc.tensor.matmul(banks[:, 0], mean_w, channel_sum, start=True, stop=True).then_inc(ln_mm, 1)
            for j in range(2, 4):
                sigmoid_tiles(j)
                head(j)
            pe.wait_ge(summed_up, 2)
            for i in range(TT):
                last = nc.tensor.matmul(banks[:, 0, i:i + 1], square_total[:, P * i:P * (i + 1)], mean_w[:, 0:1], start=True, stop=True)
            last.then_inc(ln_mm, 1)
            sigmoid_tiles(4)
            pe.wait_ge(rstd_bc_made, 1)
            for i in range(TT):
                last = nc.tensor.matmul(banks[:, 0, P * i:P * (i + 1)], ln_rstd[:, i:i + 1].to_broadcast([P, P]), ident,
                                        start=True, stop=True)
            last.then_inc(ln_mm, 1)
            sigmoid_tiles(5)
            for t in range(4):
                pe.wait_ge(sig_out[t], 7)

            def state_part(c):
                if c:
                    pe.wait_ge(ht_gated, 2 * (c - 1))
                    pe.wait_ge(kw_made, HEADS * c)
                else:
                    pe.wait_ge(head_out, HEADS + 1)
                a = chunk_span(c)[0]
                for h in range(HEADS):
                    last = nc.tensor.transpose(banks[:, 1, P * h:P * (h + 1)], k_sb[:, h, a:a + P], ident)
                last.then_inc(kt_mm, 1)
                n = P if c else META
                for h in range(HEADS):
                    pe.wait_ge(kw_made, HEADS * c + h + 1)
                    if c or h >= 2:
                        pe.wait_ge(state_out, HEADS * c + h - 1)
                    else:
                        pe.wait_ge(head_out, HEADS + 1)
                    nc.tensor.matmul(banks[:, 2 + h % 2, 0:VW], kw_sb[0:n, h], v_sb[:, c - 1, h] if c else v_meta[:, h],
                                     start=True, stop=True).then_inc(outer_mm, 1)

            whole = slice(0, SEQ)

            def pointwise(j, s):
                wait_weights(PW_PAIR + j, s)
                for c in range(GT):
                    if j:
                        pe.wait_ge(pw_out, 2 * s + c + 1)
                    channel_tile(s, c, (silu_hi, silu_lo), banks[:, PW_BANKS[2 * s + c]], whole, 3 if s else 1)

            state_part(0)
            for i in range(TT):
                pe.wait_ge(head_out, HEADS + 1)
                pe.wait_ge(tok_made, HEADS * i)
                for h in range(HEADS):
                    nc.tensor.matmul(banks[:, 4 + h, 0:VW], probs[:, h, P * i:P * (i + 1)], v_sb[:, i, h], start=True, stop=False)
                    pe.wait_ge(state_out, HEADS * i + h + 1)
                    nc.tensor.matmul(banks[:, 4 + h, 0:VW], q_sb[:, h, P * i:P * (i + 1)], state[:, h],
                                     start=False, stop=True).then_inc(h_mm, 1)
                if i + 1 < TT:
                    state_part(i + 1)
                else:
                    pe.wait_ge(state_out, HEADS * TT)
                    pe.wait_ge(silu_lo_made, KT)
                    pointwise(0, 0)
                pe.wait_ge(tok_made, HEADS * (i + 1))
                if i == 0:
                    pe.wait_ge(normed, KT)
                for f in range(2):
                    if f == 1 and i + 1 < TT:
                        pe.wait_ge(kw_made, HEADS * (i + 2))
                    if i:
                        pe.wait_ge(ht_gated, 2 * i)
                    for d in range(4):
                        hd, part = (4 * f + d) // 2, d % 2
                        last = nc.tensor.transpose(banks[:, f, P * d:P * (d + 1)], h_tok[:, hd, P * part:P * (part + 1)], ident)
                    last.then_inc(ht_mm, 1)

            for j in range(2):
                for s in range(2):
                    if j or s:
                        pointwise(j, s)
            pe.wait_ge(h_lo_made, 2 * TT)
            for j in range(2):
                for s in range(2):
                    wait_weights(OW_PAIR + j, s)
                    for c in range(GT):
                        if j:
                            pe.wait_ge(ow_out, 2 * s + c + 1)
                        elif s:
                            pe.wait_ge(pw_out, 4 + c + 1)
                        channel_tile(s, c, (h_hi, h_lo), banks[:, 2 * s + c], whole, 3 if s else 1)
            pe.wait_ge(pw_out, KT)
            for j in range(2):
                if j:
                    pe.wait_ge(ow_out, KT)
                for s in range(2):
                    wait_weights(WO_PAIR + j, s)
                    if j == 0 and s == 0:
                        for k in range(KT):
                            pe.wait_ge(mix_lo_made, k + 1)
                            for i in range(TT):
                                span = slice(P * i, P * (i + 1))
                                last = product(banks[:, 4 + i, 0:GRP], (mix_hi[:, k, span], mix_lo[:, k, span]), (w_hi[:, 0, k], w_lo[:, 0, k]), k)
                        last.then_inc(mm_done, 2)
                        continue
                    for i in range(TT):
                        token_tile(s, (mix_hi, mix_lo), banks[:, 4 * (1 - j) + i, GRP * s:GRP * (s + 1)],
                                   slice(P * i, P * (i + 1)), (3 if i == TT - 1 else 1) if s else (2 if i == TT - 1 else None))

            pe.wait_ge(router_in, 32)
            pe.wait_ge(wo_out, TT)

            def row_transposes(i):
                pe.wait_ge(u2_made, i + 1)
                for f in range(2):
                    if i >= 2:
                        pe.wait_ge(u2T_made, 2 * (i - 2) + f + 1)
                    for k in range(4):
                        col = P * (4 * f + k)
                        last = nc.tensor.transpose(banks[:, 4 * (1 - i % 2) + f, P * k:P * (k + 1)], u2[:, i % 2, col:col + P], ident)
                    last.then_inc(u2_mm, 1)

            def places(i):
                pe.wait_ge(wo_out, 2 * TT)
                pe.wait_ge(moe_consts, 2)
                pe.wait_ge(mask_made, min(i + 1, TT))
                if i >= 2:
                    pe.wait_ge(dest_made, i - 1)
                for m in range(min(i + 1, TT)):
                    last = nc.tensor.matmul(banks[:, 2 + i % 2, 0:NE], earlier if m == i else all_ones, mask[:, m],
                                            start=m == 0, stop=m == min(i, TT - 1))
                last.then_inc(place_mm, 1)

            row_transposes(0)
            for i in range(TT):
                if i + 1 < TT:
                    row_transposes(i + 1)
                pe.wait_ge(u2T_made, 2 * (i + 1))
                if i >= 2:
                    pe.wait_ge(mask_made, i - 1)
                for k in range(KT):
                    last = nc.tensor.matmul(banks[:, 6 + i % 2, 0:NE], u2T[:, i % 2, k], w_router[:, k], start=k == 0, stop=k == KT - 1)
                last.then_inc(logits_mm, 1)
                if i:
                    places(i - 1)
            places(TT - 1)
            places(TT)

            def x_transposes(n):
                pe.wait_ge(xs_in, (n + 1) * 16)
                for k in range(KT):
                    last = nc.tensor.transpose(banks[:, k // 4, SLOTS * (k % 4):SLOTS * (k % 4 + 1)], xs[:, P * k:P * (k + 1)],
                                               ident[0:SLOTS, 0:SLOTS])
                last.then_inc(xs_used, 1)

            pe.wait_ge(wo_out, 2 * TT)
            x_transposes(0)
            pe.wait_ge(bias_split, PARTS + 3)
            pe.wait_ge(passes_made, 1)
            passes = pe.value_load(n_passes[0:1, 0:1], min_val=1, max_val=PASSES)
            with pe.Fori(0, passes) as q:
                with pe.Fori(0, NE) as e:
                    n = q * NE + e

                    def hidden(k, t):
                        for g in range(CG):
                            last = nc.tensor.matmul(banks[32 * g:32 * (g + 1), t].rearrange("p (h n) -> p h n", h=2),
                                                    xT[:, k, 32 * t:32 * (t + 1)], w1_ring[k][:, :, GRP * g:GRP * (g + 1)],
                                                    start=k == 0, stop=k == KT - 1, tile_position=(0, 32 * g))
                        return last

                    pe.wait_ge(xT_made, (n + 1) * 2)
                    for k in range(KT - LATE):
                        pe.wait_ge(ring_in[k], (n + 1) * 16)
                        if k == 1:
                            pe.wait_ge(y_made, n * TG + 1)
                            pe.wait_ge(bias_made, n * 3 + 1)
                        for t in range(TG):
                            last = hidden(k, t)
                        last.then_inc(ring_used[k], 1)
                        if k == 1:
                            for m, width in ((0, 2), (1, 1)):
                                for g in range(CG):
                                    last = nc.tensor.matmul(
                                        banks[32 * g:32 * (g + 1), 3 + m, 0:GRP * width].rearrange("p (h n) -> p h n", h=width),
                                        row_pick,
                                        bias_parts[:, 2 * D * m:2 * D * m + width * D].rearrange("p (h n) -> p h n", h=width)[
                                            :, :, GRP * g:GRP * (g + 1)],
                                        start=True, stop=True, tile_position=(0, 32 * g))
                                last.then_inc(bias_mm, 1)
                    for k in range(KT - LATE, KT):
                        pe.wait_ge(ring_in[k], (n + 1) * 16)
                    for t in range(TG):
                        for k in range(KT - LATE, KT):
                            last = hidden(k, t)
                            if t == TG - 1 and k < KT - 1:
                                last.then_inc(ring_used[k], 1)
                        last.then_inc(hid_mm, 1)

                    def transposes(t):
                        pe.wait_ge(act_made, n * TG + (t + 1))
                        if t >= 2:
                            pe.wait_ge(actT_made, n * TG + (t - 1))
                        for h in range(2):
                            last = nc.tensor.transpose(banks[:, 6 + t % 2, P * h:P * (h + 1)], act_v[:, t, P * h:P * (h + 1)], ident)
                        last.then_inc(act_mm, 1)

                    def second(t):
                        pe.wait_ge(bias_made, n * 3 + 3)
                        pe.wait_ge(actT_made, n * TG + (t + 1))
                        for k in range(KT):
                            if t == 0 and k % 2 == 0:
                                pe.wait_ge(ring_in[W1C + k // 2], (n + 1) * 16)
                            for g in range(CG):
                                last = nc.tensor.matmul(banks[32 * g:32 * (g + 1), 3 + t, 0:GRP], actT[:, k, 32 * t:32 * (t + 1)],
                                                        w2_ring[k // 2][:, k % 2, GRP * g:GRP * (g + 1)],
                                                        start=k == 0, stop=k == KT - 1, tile_position=(0, 32 * g))
                            if t == TG - 1 and k % 2 == 1 and k < KT - 1:
                                last.then_inc(ring_used[W1C + k // 2], 1)
                        last.then_inc(y_mm, 1)

                    transposes(0)
                    transposes(1)
                    x_transposes(n + 1)
                    second(0)
                    transposes(2)
                    second(1)
                    second(2)

        def scale_out(dve, i):
            if i == 0:
                dve.wait_ge(last_g_in, 16)
            dve.wait_ge(rstd_made, CHUNKS + TT + i + 1)
            nc.vector.scalar_tensor_tensor(out=h_res[:, i], in0=h_res[:, i], scalar=f_rstd[:, i:i + 1], in1=last_g,
                                           op0=ALU.mult, op1=ALU.mult).then_inc(out_made, 1)

        @block.vector
        def _(dve):
            steps = [0]

            def chain(ins):
                steps[0] += 1
                ins.then_inc(dve_step, 1)
                dve.wait_ge(dve_step, steps[0])

            dve.wait_ge(g_in, 16)
            for i in range(CHUNKS):
                dve.wait_ge(rstd_made, i + 1)
                rows, n = (x_sb[:, i], P) if i < TT else (meta_sb, META)
                nc.vector.scalar_tensor_tensor(out=rows, in0=rows, scalar=row_rstd[0:n, i:i + 1], in1=g_bc[0:n],
                                               op0=ALU.mult, op1=ALU.mult).then_inc(scaled, 1)
            for j in range(2 * TT + 1):
                dve.wait_ge(u_hi_made, j + 1)
                i, h = j // 2, j % 2
                if i < TT:
                    span = (slice(None), slice(4 * h, 4 * h + 4), slice(META + P * i, META + P * (i + 1)))
                    src = banks[:, j % 4].rearrange("p (k t) -> p k t", t=P)
                else:
                    span = (slice(None), slice(None), slice(0, META))
                    src = banks[:, j % 4, 0:KT * META].rearrange("p (k t) -> p k t", t=META)
                nc.vector.tensor_tensor(u_lo[span], src, u_hi[span].bitcast(F32), ALU.subtract).then_inc(u_lo_made, 1)

            dve.wait_ge(consts_made, 6)
            for c in range(CHUNKS):
                a = chunk_span(c)[0]
                chain(nc.vector.memset(keep_row[:, a:a + 1], 0.0))
            dve.wait_ge(if_rows, 4)
            nc.vector.scalar_tensor_tensor(out=t_row, in0=f_row, scalar=-1.0, in1=f_row, op0=ALU.mult, op1=ALU.max).then_inc(abs_f, 1)
            dve.wait_ge(softplus, 1)
            chain(nc.vector.scalar_tensor_tensor(out=f_row, in0=f_row, scalar=0.0, in1=t_row, op0=ALU.min, op1=ALU.subtract))
            chain(nc.vector.tensor_tensor_scan(b_row, keep_row, f_row, 0.0, ALU.mult, ALU.add))
            chain(nc.vector.tensor_tensor(gate_rows[0:HEADS], i_row, b_row, ALU.subtract))
            chain(nc.vector.memset(m_prev[:, 0:1], 0.0))
            for c in range(CHUNKS):
                a, b = chunk_span(c)
                ar = gate_rows[0:HEADS, a:b]
                chain(nc.vector.tensor_tensor_scan(m_row[:, a:b], ar, ar, m_prev[:, c:c + 1], ALU.max, ALU.max))
                if c + 1 < CHUNKS:
                    chain(nc.vector.tensor_tensor(m_prev[:, c + 1:c + 2], b_row[:, b - 1:b], m_row[:, b - 1:b], ALU.add))
            chain(nc.vector.tensor_scalar(minus_m_end, m_row[:, META - 1::P], -1.0, None, ALU.mult))
            nc.vector.tensor_tensor(b_row, b_row, m_row, ALU.add).then_inc(m_rows, 1)

            def conv_tile(ct, first=0, end=CONV_W):
                src, one = conv_in[:, bass.ds(ct, 1), :], bass.ds(ct, 1)
                even, odd = conv[:, one, :], odd_taps.unsqueeze(1)
                for w in range(first, end):
                    if w == 0:
                        nc.vector.tensor_scalar(even, src[:, :, 0:SEQ], taps[:, one, 0], vec[:, bass.ds(ct + DW_B, 1)],
                                                ALU.mult, ALU.add).then_inc(conv_step, 1)
                        continue
                    dve.wait_ge(conv_step, ct * CONV_STEPS + max(w - 1, 1))
                    if w == 1:
                        nc.vector.tensor_scalar(odd, src[:, :, 1:1 + SEQ], taps[:, one, 1], None, ALU.mult).then_inc(conv_step, 1)
                    else:
                        to = odd if w % 2 else even
                        nc.vector.scalar_tensor_tensor(out=to, in0=src[:, :, w:w + SEQ], scalar=taps[:, one, w], in1=to,
                                                       op0=ALU.mult, op1=ALU.add).then_inc(conv_step, 1)
                if end == CONV_W:
                    dve.wait_ge(conv_step, ct * CONV_STEPS + CONV_W)
                    nc.vector.tensor_tensor(even, even, odd, ALU.add).then_inc(conv_step, 1)

            dve.wait_ge(vecs_made, 3)
            with dve.Fori(0, 4) as j:
                for c in range(GT):
                    for h in range(2):
                        dve.wait_ge(glu_sig, 4 * j + (2 * c + h + 1))
                        nc.vector.scalar_tensor_tensor(
                            out=conv_in[:, bass.ds(2 * j + c, 1), PADL + HALF * h:PADL + HALF * (h + 1)],
                            in0=banks[:, 4 * c + h:4 * c + h + 1, 0:HALF], scalar=vec[:, bass.ds(2 * j + c, 1)], in1=sg[:, h:h + 1],
                            op0=ALU.add, op1=ALU.mult).then_inc(glu_out[c], 1)
                    if c == 0:
                        dve.wait_ge(glu_out[0], 2 * j + 3)
                        conv_tile(j, 0, EARLY_TAPS)
                conv_tile(j, EARLY_TAPS, CONV_W)

            def take_v(j):
                if j == 0:
                    dve.wait_ge(vb_in, 16)
                for i in range(TT + 1):
                    dve.wait_ge(mm_done, pair_tick(V_PAIR + j, 3 + i + (i == TT)))
                    n, dst = (P, v_sb[:, i]) if i < TT else (META, v_meta)
                    nc.vector.tensor_tensor(dst[:, 2 * j:2 * j + 2, 0:DV], banks[0:n, i].rearrange("p (h v) -> p h v", v=DV),
                                            vb_bc[0:n, 512 * j:512 * (j + 1)].rearrange("p (h v) -> p h v", v=DV),
                                            ALU.add).then_inc(v_out, 1)

            dve.wait_ge(glu_out[1], 9)
            with dve.Fori(4, 6) as ct:
                conv_tile(ct)
            chain(nc.vector.memset(v_sb[:, :, :, DV:VW], 1.0))
            chain(nc.vector.memset(v_meta[:, :, DV:VW], 1.0))
            take_v(0)
            conv_tile(6)
            take_v(1)
            conv_tile(7)

            dve.wait_ge(conv_step, CONV_STEPS * KT)
            nc.vector.tensor_reduce(channel_sum, conv.rearrange("p k t -> p t k"), axis=AX.X, op=ALU.add).then_inc(summed_up, 1)

            def head_probs(h):
                one = bass.ds(h, 1)
                dve.wait_ge(head_mm, h + 1)
                for i in range(TT):
                    nc.vector.scalar_tensor_tensor(out=probs[:, one, P * i:P * (i + 1)], in0=banks[:, 1:2, P * i:P * (i + 1)],
                                                   scalar=cols[:, i + 1, one], in1=maskpos.unsqueeze(1), op0=ALU.subtract,
                                                   op1=ALU.max).then_inc(e_made, 1)
                nc.vector.tensor_copy(decay[:, one], banks[:, 2:3, P - 1::P])
                nc.vector.tensor_tensor(q_sb[:, one], q_sb[:, one], banks[:, 2:3], ALU.mult)
                dve.wait_ge(d_made, h + 1)
                nc.vector.tensor_tensor(probs[:, one], probs[:, one], banks[:, 3:4], ALU.mult).then_inc(head_out, 1)

            dve.wait_ge(cols_made, 1)
            with dve.Fori(0, 2) as h:
                head_probs(h)
            dve.wait_ge(ln_mm, 1)
            nc.vector.tensor_tensor(conv, conv, banks[:, 0:1].to_broadcast([P, KT, SEQ]), ALU.subtract).then_inc(centered, 1)
            dve.wait_ge(squares_made, 1)
            nc.vector.tensor_reduce(square_total, squares.rearrange("p k t -> p t k"), axis=AX.X, op=ALU.add).then_inc(summed_up, 1)
            with dve.Fori(2, 4) as h:
                head_probs(h)
            dve.wait_ge(ln_mm, 2)
            nc.vector.tensor_scalar(ln_rstd, banks[:, 0, 0:TT], EPS, None, ALU.add).then_inc(var_made, 1)
            dve.wait_ge(ln_mm, 3)
            for k in range(KT):
                nc.vector.tensor_tensor(conv[:, k], conv[:, k], banks[:, 0], ALU.mult).then_inc(normed, 1)

            def update_state(c):
                for h in range(HEADS):
                    dve.wait_ge(outer_mm, HEADS * c + h + 1)
                    src = banks[:, 2 + h % 2, 0:VW]
                    if c == 0:
                        nc.vector.tensor_copy(state[:, h], src).then_inc(state_out, 1)
                    else:
                        dve.wait_ge(h_mm, HEADS * (c - 1) + h + 1)
                        nc.vector.scalar_tensor_tensor(out=state[:, h], in0=state[:, h], scalar=decay[:, h, c - 1:c], in1=src,
                                                       op0=ALU.mult, op1=ALU.add).then_inc(state_out, 1)

            update_state(0)
            for i in range(TT):
                dve.wait_ge(h_mm, HEADS * (i + 1))
                dve.wait_ge(h_squared, HEADS * i)
                dve.wait_ge(h_scaled, i)
                den = banks[:, 4:8, DV:VW].rearrange("p h v -> p (h v)")
                chain(nc.vector.scalar_tensor_tensor(out=den_inv, in0=den, scalar=-1.0, in1=cols[:, i + 1, FLOOR_ROW:FLOOR_ROW + HEADS],
                                                     op0=ALU.mult, op1=ALU.max))
                chain(nc.vector.tensor_tensor(den_inv, den_inv, den, ALU.max))
                nc.vector.reciprocal(den_inv, den_inv).then_inc(den_made, 1)
                if i + 1 < TT:
                    update_state(i + 1)
                for f in range(2):
                    dve.wait_ge(ht_mm, 2 * i + f + 1)
                    dve.wait_ge(og_made, KT)
                    og = gates[:, OG + 4 * f:OG + 4 * f + 4, P * i:P * (i + 1)]
                    nc.vector.tensor_tensor(og, og, banks[:, f].rearrange("p (d t) -> p d t", t=P), ALU.mult).then_inc(ht_gated, 1)
                for f in range(2):
                    dve.wait_ge(h_hi_made, 2 * i + f + 1)
                    span = (slice(None), slice(4 * f, 4 * f + 4), slice(P * i, P * (i + 1)))
                    nc.vector.tensor_tensor(h_lo[span], gates[:, OG:OG + KT][span], h_hi[span].bitcast(F32),
                                            ALU.subtract).then_inc(h_lo_made, 1)
                for k in SILU_TILES[i]:
                    dve.wait_ge(silu_hi_made, k + 1)
                    nc.vector.tensor_tensor(silu_lo[:, k], conv[:, k], silu_hi[:, k].bitcast(F32), ALU.subtract).then_inc(silu_lo_made, 1)
            for j in range(2):
                for t in range(4):
                    dve.wait_ge(mm_done, pair_tick(PW_PAIR + j, (1 + t) if t < 2 else 3 * t - 1))
                    g = gates[:, GC + 4 * j + t]
                    nc.vector.scalar_tensor_tensor(out=g, in0=banks[:, PW_BANKS[t]], scalar=vec[:, PW_B + 4 * j + t:PW_B + 4 * j + t + 1],
                                                   in1=g, op0=ALU.add, op1=ALU.mult).then_inc(pw_out, 1)
            for j in range(2):
                for t in range(4):
                    n = 4 * j + t
                    dve.wait_ge(mm_done, pair_tick(OW_PAIR + j, (1 + t) if t < 2 else 3 * t - 1))
                    g, m = gates[:, GC + n], gates[:, GM + n]
                    nc.vector.tensor_tensor(m, m, banks[:, t], ALU.mult).then_inc(ow_out, 1)
                    dve.wait_ge(ow_out, n + 1)
                    nc.vector.tensor_tensor(g, g, m, ALU.add).then_inc(mixed, 1)
                    dve.wait_ge(mix_hi_made, n + 1)
                    nc.vector.tensor_tensor(mix_lo[:, n], g, mix_hi[:, n].bitcast(F32), ALU.subtract).then_inc(mix_lo_made, 1)
            dve.wait_ge(res_in, 16)
            for j in range(2):
                for i in range(TT):
                    dve.wait_ge(mm_done, pair_tick(WO_PAIR + j, 3 + i if i < TT - 1 else 8))
                    r = h_res[:, i, 512 * j:512 * (j + 1)]
                    nc.vector.tensor_tensor(r, r, banks[:, 4 * (1 - j) + i], ALU.add).then_inc(wo_out, 1)

            dve.wait_ge(gf_in, 16)
            for i in range(TT):
                dve.wait_ge(rstd_made, CHUNKS + i + 1)
                nc.vector.scalar_tensor_tensor(out=u2[:, i % 2], in0=h_res[:, i], scalar=h_rstd[:, i:i + 1], in1=gf_bc,
                                               op0=ALU.mult, op1=ALU.mult).then_inc(u2_made, 1)
            dve.wait_ge(router_in, 32)
            dve.wait_ge(moe_consts, 2)

            def choose(i):
                dve.wait_ge(logits_mm, i + 1)
                chain(nc.vector.tensor_tensor(logits[:, i], banks[:, 6 + i % 2, 0:NE], rb_bc, ALU.add))
                chain(nc.vector.max(best[:, i], logits[:, i]))
                chain(nc.vector.max_index(best_idx[:, i], best[:, i], logits[:, i]))
                chain(nc.vector.tensor_copy(expert_f[:, i], best_idx[:, i, 0:TOPK]))
                chain(nc.vector.tensor_tensor(one_hot[:, i], expert_id.unsqueeze(1).to_broadcast([P, TOPK, NE]),
                                              expert_f[:, i].unsqueeze(2).to_broadcast([P, TOPK, NE]), ALU.is_equal))
                with nc.allow_low_precision(reason="ones and zeros"):
                    nc.vector.tensor_reduce(mask[:, i], one_hot[:, i].rearrange("p k e -> p e k"), axis=AX.X, op=ALU.add).then_inc(mask_made, 1)

            def find_slots(i):
                dve.wait_ge(place_mm, i + 1)
                chain(nc.vector.tensor_tensor(picked[:, i], one_hot[:, i], banks[:, 2 + i % 2, 0:NE].unsqueeze(1).to_broadcast([P, TOPK, NE]),
                                              ALU.mult))
                chain(nc.vector.tensor_reduce(place[:, i], picked[:, i], axis=AX.X, op=ALU.add))
                nc.vector.scalar_tensor_tensor(out=dest[:, TOPK * i:TOPK * (i + 1)], in0=place[:, i], scalar=float(NE), in1=expert_f[:, i],
                                               op0=ALU.mult, op1=ALU.add).then_inc(dest_made, 1)

            for i in range(TT):
                choose(i)
                if i:
                    find_slots(i - 1)
            find_slots(TT - 1)
            nc.vector.tensor_tensor(gate_w, best[:, :, 0:TOPK], best[:, :, 0:1].to_broadcast([P, TT, TOPK]), ALU.subtract).then_inc(shifted, 1)
            dve.wait_ge(place_mm, TT + 1)
            chain(nc.vector.reduce_max(count_max, banks[:, 2 + TT % 2, 0:NE], axis=AX.X))
            chain(nc.vector.tensor_scalar(over[:, 0:PASSES - 1], steps96, count_max, None, ALU.is_lt))
            chain(nc.vector.tensor_reduce(count_max, over[:, 0:PASSES - 1], axis=AX.X, op=ALU.add))
            nc.vector.tensor_scalar(n_passes, count_max, 1.0, None, ALU.add).then_inc(passes_made, 1)
            dve.wait_ge(bias_split, 1)
            nc.vector.tensor_tensor(bias_rest, bias_rest, bias_parts, ALU.subtract).then_inc(bias_split, 1)
            dve.wait_ge(gate_exp, 1)
            chain(nc.vector.tensor_reduce(gate_sum, gate_w, axis=AX.X, op=ALU.add))
            chain(nc.vector.reciprocal(gate_sum, gate_sum))
            chain(nc.vector.tensor_tensor(gate_w, gate_w, gate_sum.unsqueeze(2).to_broadcast([P, TT, TOPK]), ALU.mult))
            dve.wait_ge(bias_split, PARTS + 1)
            nc.vector.tensor_tensor(bias_rest[last_part], bias_rest[last_part], bias_parts[last_part], ALU.subtract).then_inc(bias_split, 1)
            dve.wait_ge(table_in, 16)
            nc.vector.tensor_scalar(token_of, token_of, 2, None, ALU.arith_shift_right).then_inc(tables_made, 1)
            dve.wait_ge(rows_in, 16 * CG * TG)
            nc.vector.tensor_scalar(row_of, row_of, float(CG), group_of, ALU.mult, ALU.add).then_inc(tables_made, 1)

            passes = dve.value_load(n_passes[0:1, 0:1], min_val=1, max_val=PASSES)
            STEPS = 3 * TG
            with dve.Fori(0, passes) as q:
                with dve.Fori(0, NE) as e:
                    n = q * NE + e
                    k = [0]

                    def own(ins):
                        k[0] += 1
                        ins.then_inc(ffn_step, 1)
                        dve.wait_ge(ffn_step, n * STEPS + k[0])

                    def clamped(t):
                        dve.wait_ge(hid_mm, n * TG + (t + 1))
                        own(nc.vector.tensor_tensor(hid[:, t], banks[:, t], bias1.rearrange("p h n -> p (h n)"), ALU.add))
                        nc.vector.tensor_scalar(hid[:, t, 0:GRP], hid[:, t, 0:GRP], LIMIT, None, ALU.min).then_inc(glu_made, 1)
                        own(nc.vector.tensor_scalar(hid[:, t, GRP:2 * GRP], hid[:, t, GRP:2 * GRP], LIMIT, -LIMIT, ALU.min, ALU.max))

                    def activated(t):
                        lin = hid[:, t, GRP:2 * GRP]
                        dve.wait_ge(glu_made, n * TG + (t + 1))
                        own(nc.vector.scalar_tensor_tensor(out=lin, in0=lin, scalar=1.0, in1=hid[:, t, 0:GRP], op0=ALU.add, op1=ALU.mult))
                        dve.wait_ge(sig_made, n * TG + (t + 1))
                        nc.vector.tensor_tensor(act_v[:, t], lin, sig[:, t], ALU.mult).then_inc(act_made, 1)

                    dve.wait_ge(bias_made, n * 3 + 2)
                    for t in range(TG):
                        clamped(t)
                        activated(t)
                    assert k[0] == STEPS
                    dve.wait_ge(bias_made, n * 3 + 3)
                    dve.wait_ge(idx_step, n * IDX + 5)
                    for t in range(TG):
                        dve.wait_ge(y_mm, n * TG + (t + 1))
                        nc.vector.tensor_tensor(y_out[:, t], banks[:, 3 + t, 0:GRP], bias2, ALU.add).then_inc(y_made, 1)
            for i in range(TT):
                dve.wait_ge(y_loaded[i], 16)
                for j in range(TOPK):
                    if i == TT - 1 and j == 2:
                        dve.wait_ge(y_loaded[TT], 16)
                    ins = nc.vector.scalar_tensor_tensor(out=h_res[:, i], in0=y_in[:, i, j], scalar=gate_w[:, i, j:j + 1], in1=h_res[:, i],
                                                         op0=ALU.mult, op1=ALU.add)
                    if j < TOPK - 1:
                        chain(ins)
                    else:
                        ins.then_inc(summed, 1)
                if i:
                    scale_out(dve, i - 1)
            scale_out(dve, TT - 1)


_INS = ['x', 'meta_tokens', 'norm_mix_g', 'w_in', 'b_in', 'conv_dw_w', 'conv_dw_b', 'conv_ln_g', 'conv_ln_b',
        'conv_pw_w', 'conv_pw_b', 'mlstm_norm_g', 'mlstm_out_w', 'w_out', 'norm_ffn_g', 'router_w', 'router_b',
        'expert_w1', 'expert_b1', 'expert_w2', 'expert_b2', 'final_norm_g']
_OUTS = [((1, SEQ, D), 'float32')]


def kernel(**inputs):
    import numpy as _np
    import concourse.bacc as _bacc
    from concourse import mybir as _mybir
    from concourse.bass_utils import run_bass_kernel_spmd as _run

    nc = _bacc.Bacc("TRN2", target_bir_lowering=False, num_devices=1)
    arrays, args = {}, []
    for name in _INS:
        a = _np.ascontiguousarray(inputs[name])
        arrays[f"in_{name}_dram"] = a
        args.append(nc.dram_tensor(f"in_{name}_dram", a.shape, _mybir.dt.from_np(a.dtype), kind="ExternalInput").ap())
    for i, (shape, dtype) in enumerate(_OUTS):
        dt = _mybir.dt.from_np(_np.dtype(dtype))
        args.append(nc.dram_tensor(f"out_{i}_dram", shape, dt, kind="ExternalOutput").ap())
    hybrid_block(nc, *args)
    r = _run(nc, [arrays], core_ids=[0])
    return r.results[0]["out_0_dram"]
```
